# Optimizing a Trainium2 kernel written in Bass

```python
import jax, jax.numpy as jnp
from jax import lax
import numpy as np

D_MODEL = 1024
BATCH = 1
SEQ = 1024
DEPTH = 1

CHUNK = 64
WINDOW = 128
WIN_CHUNKS = WINDOW // CHUNK
A_HEADS = 8
A_KV_HEADS = 2
A_HEAD_DIM = 64
A_GROUP = A_HEADS // A_KV_HEADS
B_HEADS = 8
B_Q_RANK = 256
B_KV_RANK = 128
B_NOPE_DIM = 64
B_ROPE_DIM = 32
B_V_DIM = 64
B_QK_DIM = B_NOPE_DIM + B_ROPE_DIM
ROPE_THETA = 10000.0
Q_BLOCK = 128
D_FF = 4 * D_MODEL
N_BRANCH = 2
EPS = 1e-6

A_Q_COLS = A_HEADS * A_HEAD_DIM
A_KV_COLS = A_KV_HEADS * A_HEAD_DIM
GATE_COLS = N_BRANCH * D_MODEL
COL_SIZES = [A_Q_COLS, A_KV_COLS, A_KV_COLS, B_Q_RANK, B_KV_RANK, B_ROPE_DIM, GATE_COLS]
COL_SPLITS = [int(v) for v in np.cumsum(COL_SIZES)[:-1]]
IN_COLS = int(sum(COL_SIZES))
A_OUT = A_HEADS * A_HEAD_DIM
B_OUT = B_HEADS * B_V_DIM

kernel_name = "hybrid_swa_sink_mla_gated_block"

def rms_norm(x, g):
    xf = x.astype(jnp.float32)
    y = xf * lax.rsqrt(jnp.mean(xf * xf, axis=-1, keepdims=True) + EPS)
    return (y * g.astype(jnp.float32)).astype(x.dtype)

def alibi_slopes(n_heads):
    return jnp.exp2(-8.0 * jnp.arange(1, n_heads + 1, dtype=jnp.float32) / n_heads)

def rope(x, pos):
    half = B_ROPE_DIM // 2
    inv = ROPE_THETA ** (-jnp.arange(half, dtype=jnp.float32) / half)
    ang = pos.astype(jnp.float32)[..., None] * inv
    ang = ang.reshape(ang.shape[:2] + (1,) * (x.ndim - 3) + (half,))
    cos, sin = jnp.cos(ang), jnp.sin(ang)
    xf = x.astype(jnp.float32)
    x1, x2 = xf[..., :half], xf[..., half:]
    return jnp.concatenate([x1 * cos - x2 * sin, x2 * cos + x1 * sin], axis=-1).astype(x.dtype)

def band_chunks(t, nc):
    tc = t.reshape((t.shape[0], nc, CHUNK) + t.shape[2:])
    pad = WIN_CHUNKS - 1
    tp = jnp.pad(tc, [(0, 0), (pad, 0)] + [(0, 0)] * (tc.ndim - 2))
    return jnp.concatenate([tp[:, j:j + nc] for j in range(WIN_CHUNKS)], axis=2)

def swa_sink_attention(q, k, v, pos, g_q, g_k, sinks):
    Bn, S = q.shape[:2]
    nc = S // CHUNK
    q = rms_norm(q, g_q)
    k = rms_norm(k, g_k)
    qb = q.reshape(Bn, nc, CHUNK, A_KV_HEADS, A_GROUP, A_HEAD_DIM)
    kb = band_chunks(k, nc)
    vb = band_chunks(v, nc)
    pk = band_chunks(pos, nc)
    pq = pos.reshape(Bn, nc, CHUNK)
    n_keys = WIN_CHUNKS * CHUNK
    valid = (jnp.arange(nc)[:, None] + jnp.arange(n_keys)[None, :] // CHUNK) >= (WIN_CHUNKS - 1)
    s = jnp.einsum('bcqhgd,bckhd->bchgqk', qb, kb).astype(jnp.float32) * (A_HEAD_DIM ** -0.5)
    dist = jnp.abs(pq[:, :, :, None] - pk[:, :, None, :]).astype(jnp.float32)
    slopes = alibi_slopes(A_HEADS).reshape(A_KV_HEADS, A_GROUP)
    s = s - slopes[None, None, :, :, None, None] * dist[:, :, None, None, :, :]
    s = jnp.where(valid[None, :, None, None, None, :], s, -jnp.inf)
    sink = sinks.astype(jnp.float32).reshape(A_KV_HEADS, A_GROUP)[None, None, :, :, None, None]
    m = jnp.maximum(jnp.max(s, axis=-1, keepdims=True), sink)
    p = jnp.exp(s - m)
    p = p / (jnp.sum(p, axis=-1, keepdims=True) + jnp.exp(sink - m))
    o = jnp.einsum('bchgqk,bckhd->bcqhgd', p.astype(v.dtype), vb)
    return o.reshape(Bn, S, A_OUT)

def mla_attention(c_q, c_kv, k_rope, pos, g_cq, g_ckv, w_uq, w_ukv, g_q, g_k):
    Bn, S = c_q.shape[:2]
    q = (rms_norm(c_q, g_cq) @ w_uq).reshape(Bn, S, B_HEADS, B_QK_DIM)
    kv = (rms_norm(c_kv, g_ckv) @ w_ukv).reshape(Bn, S, B_HEADS, B_NOPE_DIM + B_V_DIM)
    k_nope, v = kv[..., :B_NOPE_DIM], kv[..., B_NOPE_DIM:]
    k_r = jnp.broadcast_to(k_rope[:, :, None, :], (Bn, S, B_HEADS, B_ROPE_DIM))
    k = jnp.concatenate([k_nope, k_r], axis=-1)
    q = rms_norm(q, g_q)
    k = rms_norm(k, g_k)
    q = jnp.concatenate([q[..., :B_NOPE_DIM], rope(q[..., B_NOPE_DIM:], pos)], axis=-1)
    k = jnp.concatenate([k[..., :B_NOPE_DIM], rope(k[..., B_NOPE_DIM:], pos)], axis=-1)
    nb = S // Q_BLOCK
    qb = q.reshape(Bn, nb, Q_BLOCK, B_HEADS, B_QK_DIM).transpose(1, 0, 2, 3, 4)
    key_chunk = jnp.arange(S) // CHUNK
    scale = B_QK_DIM ** -0.5

    def block(args):
        qi, i = args
        q_chunk = (i * Q_BLOCK + jnp.arange(Q_BLOCK)) // CHUNK
        s = jnp.einsum('bqhd,bkhd->bhqk', qi, k).astype(jnp.float32) * scale
        s = jnp.where(key_chunk[None, :] <= q_chunk[:, None], s, -jnp.inf)
        p = jax.nn.softmax(s, axis=-1).astype(v.dtype)
        return jnp.einsum('bhqk,bkhd->bqhd', p, v)

    o = lax.map(block, (qb, jnp.arange(nb)))
    return o.transpose(1, 0, 2, 3, 4).reshape(Bn, S, B_OUT)

def setup_inputs(seed: int = 0) -> dict:
    key = jax.random.key(seed)
    ks = jax.random.split(key, 24)
    f32 = jnp.float32

    def nrm(k, shape, scale):
        return jax.random.normal(k, shape, f32) * scale

    def gain(k, dim):
        return 1.0 + 0.02 * jax.random.normal(k, (DEPTH, dim), f32)

    offs = jax.random.randint(ks[1], (BATCH, 1), 0, 64, dtype=jnp.int32) * CHUNK
    positions = (offs + jnp.arange(SEQ, dtype=jnp.int32)[None, :]).astype(jnp.int32)
    return {
        "x": nrm(ks[0], (BATCH, SEQ, D_MODEL), 1.0),
        "positions": positions,
        "g_mix": gain(ks[2], D_MODEL),
        "w_in": nrm(ks[3], (DEPTH, D_MODEL, IN_COLS), D_MODEL ** -0.5),
        "b_gate": nrm(ks[4], (DEPTH, GATE_COLS), 0.1),
        "g_qa": gain(ks[5], A_HEAD_DIM),
        "g_ka": gain(ks[6], A_HEAD_DIM),
        "sinks_a": nrm(ks[7], (DEPTH, A_HEADS), 0.5),
        "g_cq": gain(ks[8], B_Q_RANK),
        "g_ckv": gain(ks[9], B_KV_RANK),
        "w_uq": nrm(ks[10], (DEPTH, B_Q_RANK, B_HEADS * B_QK_DIM), B_Q_RANK ** -0.5),
        "w_ukv": nrm(ks[11], (DEPTH, B_KV_RANK, B_HEADS * (B_NOPE_DIM + B_V_DIM)), B_KV_RANK ** -0.5),
        "g_qb": gain(ks[12], B_QK_DIM),
        "g_kb": gain(ks[13], B_QK_DIM),
        "w_branch_a": nrm(ks[14], (DEPTH, A_OUT, D_MODEL), A_OUT ** -0.5),
        "w_branch_b": nrm(ks[15], (DEPTH, B_OUT, D_MODEL), B_OUT ** -0.5),
        "w_out": nrm(ks[16], (DEPTH, D_MODEL, D_MODEL), D_MODEL ** -0.5),
        "g_mlp": gain(ks[17], D_MODEL),
        "w_ff1": nrm(ks[18], (DEPTH, D_MODEL, D_FF), D_MODEL ** -0.5),
        "w_ff2": nrm(ks[19], (DEPTH, D_FF, D_MODEL), D_FF ** -0.5),
    }

def reference(x, positions, g_mix, w_in, b_gate, g_qa, g_ka, sinks_a, g_cq, g_ckv,
              w_uq, w_ukv, g_qb, g_kb, w_branch_a, w_branch_b, w_out, g_mlp, w_ff1, w_ff2):
    Bn, S = x.shape[:2]
    for l in range(DEPTH):
        h = rms_norm(x, g_mix[l])
        z = h @ w_in[l]
        qa, ka, va, cq, ckv, krope, gates = jnp.split(z, COL_SPLITS, axis=-1)
        y_a = swa_sink_attention(
            qa.reshape(Bn, S, A_HEADS, A_HEAD_DIM),
            ka.reshape(Bn, S, A_KV_HEADS, A_HEAD_DIM),
            va.reshape(Bn, S, A_KV_HEADS, A_HEAD_DIM),
            positions, g_qa[l], g_ka[l], sinks_a[l])
        y_b = mla_attention(cq, ckv, krope, positions, g_cq[l], g_ckv[l],
                            w_uq[l], w_ukv[l], g_qb[l], g_kb[l])
        gt = jax.nn.sigmoid((gates + b_gate[l]).astype(jnp.float32)).astype(x.dtype)
        gt = gt.reshape(Bn, S, N_BRANCH, D_MODEL)
        merged = gt[:, :, 0] * (y_a @ w_branch_a[l]) + gt[:, :, 1] * (y_b @ w_branch_b[l])
        x = x + merged @ w_out[l]
        h2 = rms_norm(x, g_mlp[l])
        x = x + jnp.square(jax.nn.relu(h2 @ w_ff1[l])) @ w_ff2[l]
    return x


_drawn_inputs = setup_inputs


def setup_inputs(seed=0):
    import zlib

    import numpy as np

    out = dict(_drawn_inputs(seed))
    spreads = {}
    factors = {'g_mix': 8.0,
     'b_gate': 8.0,
     'g_qa': 8.0,
     'g_ka': 8.0,
     'sinks_a': 8.0,
     'g_cq': 8.0,
     'g_ckv': 8.0,
     'g_qb': 8.0,
     'g_kb': 8.0,
     'g_mlp': 9.264}
    for name, (base, spread) in spreads.items():
        noise = np.random.default_rng([zlib.crc32(name.encode()), seed]).standard_normal(out[name].shape)
        drawn = base * np.exp(spread * noise) if base else spread * noise
        out[name] = __import__('jax').numpy.asarray(drawn.astype(out[name].dtype))
    for name, factor in factors.items():
        out[name] = (out[name] * factor).astype(out[name].dtype)
    return out
```

```python
from contextlib import ExitStack

import numpy as np
import concourse.bass as bass
from concourse import mybir

F32 = mybir.dt.float32
F32R = mybir.dt.float32r
I32 = mybir.dt.int32
ACT = mybir.ActivationFunctionType
ALU = mybir.AluOpType
AX = mybir.AxisListType

P = 128
S = 1024
D = 1024
T = S // P
KD = D // P
HALF = S // 2
EPS = 1e-6

A_HEADS, A_KV, A_DIM = 8, 2, 64
A_GROUP = A_HEADS // A_KV
CHUNK = 64
WIN = 3 * CHUNK
B_HEADS, NOPE, ROPE, V_DIM = 8, 64, 32, 64
QK = NOPE + ROPE
RH = ROPE // 2
B_GROUP = 4
B_GROUPS = B_HEADS // B_GROUP
Q_RANK, KV_RANK = 256, 128
D_FF = 4 * D

C_Q, C_K, C_V = 0, 512, 640
C_CQ, C_CKV, C_KR = 768, 1024, 1152
Z_COLS = 1184
Z_CHUNKS = 4
ZC = Z_COLS // Z_CHUNKS
N_STAT = A_HEADS + A_KV + 3
ST_CQ, ST_CKV, ST_KR = 10, 11, 12

GROUP = 4
FF_GROUPS = D_FF // P // GROUP
MASKED = 1e30
SLOPES = [float(2.0 ** (-8.0 * (h + 1) / A_HEADS)) for h in range(A_HEADS)]
INV_FREQ = (np.float32(10000.0) ** (-np.arange(RH, dtype=np.float32) / np.float32(RH))).tolist()
TWO_PI = 2.0 * np.pi
PI_A = float(np.float32(6.28125))
PI_B = float(np.float32(np.round((TWO_PI - PI_A) * 2 ** 20) / 2 ** 20))
PI_C = float(np.float32(TWO_PI - PI_A - PI_B))
ROUND = float(1.5 * 2 ** 23)
SIN_MAX = 3.1415925


def build(nc, x, positions, g_mix, w_in, b_gate, g_qa, g_ka, sinks_a, g_cq, g_ckv,
          w_uq, w_ukv, g_qb, g_kb, w_branch_a, w_branch_b, w_out, g_mlp, w_ff1, w_ff2, out):
    x_d = x[0].rearrange("(t p) d -> t p d", p=P)
    out_d = out[0].rearrange("(t p) d -> t p d", p=P)
    w_in_d, w_uq_d, w_ukv_d = w_in[0], w_uq[0], w_ukv[0]
    w_out_d, w1_d, w2_d = w_out[0], w_ff1[0], w_ff2[0]

    with ExitStack() as ctx:
        def sem(name):
            return ctx.enter_context(nc.semaphore(name))

        def const(name, shape, dt=F32):
            return ctx.enter_context(nc.sbuf_tensor(name, shape, dt))

        ident = const("ident", [P, P])
        g_mix_c = const("g_mix_c", [P, KD])
        g_mlp_c = const("g_mlp_c", [P, KD])
        b_gate_c = const("b_gate_c", [P, 2 * KD])
        g_qa_c = const("g_qa_c", [P, 1])
        g_ka_c = const("g_ka_c", [P, 1])
        gqk_a = const("gqk_a", [P, 1])
        g_cq_c = const("g_cq_c", [P, 2])
        g_ckv_c = const("g_ckv_c", [P, 1])
        g_qb_c = const("g_qb_c", [P, 1])
        g_kb_c = const("g_kb_c", [P, 1])
        gqk_b = const("gqk_b", [P, 1])
        g_qr = const("g_qr", [P, ROPE])
        g_kr = const("g_kr", [P, ROPE])
        sink_r = const("sink_r", [P, A_HEADS])
        pos_i = const("pos_i", [P, T], I32)
        pos_c = const("pos_c", [P, T])
        inv_f = const("inv_f", [P, RH])
        minus_half = const("minus_half", [P, T * N_STAT])
        x_ss = const("x_ss", [P, T])
        x_ms = const("x_ms", [P, T])
        x_rstd = const("x_rstd", [P, T])
        z_ss = const("z_ss", [P, T, N_STAT])
        z_ms = const("z_ms", [P, T, N_STAT])
        z_rstd = const("z_rstd", [P, T, N_STAT])
        b_ss = const("b_ss", [P, 4, 2 * B_GROUP])
        b_ms = const("b_ms", [P, 4, 2 * B_GROUP])
        b_rstd = const("b_rstd", [P, 4, 2 * B_GROUP])
        cos_t = const("cos_t", [P, T, RH])
        sin_t = const("sin_t", [P, T, RH])
        kr_rot = const("kr_rot", [P, T, ROPE])
        a_nmax = const("a_nmax", [P, 2, A_GROUP])
        a_sum = const("a_sum", [P, 2, A_GROUP])
        a_rsum = const("a_rsum", [P, 2, A_GROUP])
        b_nmax = const("b_nmax", [P, 2])
        b_sum = const("b_sum", [P, 2])
        b_rsum = const("b_rsum", [P, 2])

        BASE = 8
        probe = ctx.enter_context(nc.sbuf_tensor("base_gap", [P, 8], F32))
        used = 0
        for t_ in (ident, g_mix_c, g_mlp_c, b_gate_c, g_qa_c, g_ka_c, gqk_a, g_cq_c, g_ckv_c, g_qb_c, g_kb_c,
                   gqk_b, g_qr, g_kr, sink_r, pos_i, pos_c, inv_f, minus_half, x_ss, x_ms, x_rstd, z_ss, z_ms,
                   z_rstd, b_ss, b_ms, b_rstd, cos_t, sin_t, kr_rot, a_nmax, a_sum, a_rsum, b_nmax, b_sum,
                   b_rsum, probe):
            n = 4
            for v in t_.shape[1:]:
                n *= v
            used += (n + 31) // 32 * 32
        assert used <= BASE * 1024, used

        def place(name, kib, shape, dt=F32):
            pad = int(kib * 1024) - used
            with nc.sbuf_tensor("pad_" + name, [P, pad // 4], F32):
                with nc.sbuf_tensor(name, shape, dt) as t_:
                    return t_

        hT_hi = place("hT_hi", 8, [P, KD, S], F32R)
        hT_lo = place("hT_lo", 40, [P, KD, S], F32R)
        x_in = place("x_in", 72, [P, T, D])
        zw_hi = [place(f"zw_hi{i}", 104 + 18.5 * i, [P, KD, ZC], F32R) for i in range(2)]
        zw_lo = [place(f"zw_lo{i}", 113.25 + 18.5 * i, [P, KD, ZC], F32R) for i in range(2)]
        z_raw = [place(f"z_raw{i}", 141 + 4.625 * i, [P, 4, ZC]) for i in range(4)]
        sq = place("sq", 160, [P, Z_COLS])
        Z = place("Z", 168, [P, T, Z_COLS])
        gw_hi = [place(f"gw_hi{i}", 72 + 8 * i, [P, KD, P], F32R) for i in range(2)]
        gw_lo = [place(f"gw_lo{i}", 76 + 8 * i, [P, KD, P], F32R) for i in range(2)]
        gate = place("gate", 88, [P, 2 * KD, S])
        g_raw = [place(f"g_raw{i}", 152 + 4 * i, [P, KD, P]) for i in range(2)]
        k_dup = place("k_dup", 160, [P, T, A_KV, 2, A_DIM])
        rope_tmp = [place(f"rope_tmp{i}", 165 + 0.5 * i, [P, T, RH]) for i in range(6)]
        qaT = place("qaT", 8, [P, 4, S])
        kaT = place("kaT", 24, [P, A_KV, CHUNK + S])
        dist = place("dist", 32.5, [P, T, WIN])
        scA = place("scA", 38.5, [P, 2, A_GROUP, WIN + 2])
        ptA_full = [place(f"ptA_full{i}", 45 + 4 * i, [P, A_GROUP, P]) for i in range(2)]
        ptA_half = [place(f"ptA_half{i}", 47 + 4 * i, [P, A_GROUP, P]) for i in range(2)]
        v_odd = place("v_odd", 53, [P, T, A_KV * A_DIM])
        cqT = place("cqT", 59, [P, 2, S])
        ckvT = place("ckvT", 67, [P, S])
        wuq = place("wuq", 71, [P, 2, B_GROUP * QK])
        wukv = place("wukv", 74, [P, B_GROUP * (NOPE + V_DIM)])
        pos_row_i = place("pos_row_i", 76, [P, S], I32)
        pos_row = place("pos_row", 80, [P, CHUNK + S])
        yA = place("yA", 152, [P, T, A_HEADS * A_DIM])
        yB = place("yB", 8, [P, T, B_HEADS * V_DIM])
        qbT = place("qbT", 24, [P, B_GROUP, S])
        kbT = place("kbT", 40, [P, B_GROUP, S])
        sqB = place("sqB", 56, [P, B_GROUP * (QK + NOPE)])
        vB = place("vB", 76, [P, T, B_GROUP, V_DIM])
        q_nat = [place(f"q_nat{i}", 168 + 6 * i, [P, 4, B_GROUP, QK]) for i in range(2)]
        k_nat = [place(f"k_nat{i}", 180 + 6 * i, [P, 4, B_GROUP, QK]) for i in range(2)]
        rtmp = [place(f"rtmp{i}", 192 + i, [P, 4, B_GROUP, RH]) for i in range(4)]
        ptB = [place(f"ptB{i}", 168 + 4 * i, [P, T, P]) for i in range(2)]
        prB = [place(f"prB{i}", 176 + 4 * i, [P, S]) for i in range(2)]
        yT_hi = place("yT_hi", 24, [P, 8, S], F32R)
        yT_lo = place("yT_lo", 56, [P, 8, S], F32R)
        raw = [place(f"raw{i}", 192 + 4 * i, [P, 1024]) for i in range(2)]
        bw_at = [184, 168]
        bw_hi = [place(f"bw_hi{i}", bw_at[i], [P, 8, P], F32R) for i in range(2)]
        bw_lo = [place(f"bw_lo{i}", bw_at[i] + 4, [P, 8, P], F32R) for i in range(2)]
        gated_a = place("gated_a", 176, [P, S])
        gated_b = place("gated_b", 180, [P, S])
        merged = place("merged", 200, [P, S])
        mT_hi = place("mT_hi", 88, [P, KD, S], F32R)
        mT_lo = place("mT_lo", 120, [P, KD, S], F32R)
        ow_at = [8, 16, 152, 160, 24, 32, 40, 48]
        ow_hi = [place(f"ow_hi{i}", ow_at[i], [P, D], F32R) for i in range(8)]
        ow_lo = [place(f"ow_lo{i}", ow_at[i] + 4, [P, D], F32R) for i in range(8)]
        xr = place("xr", 56, [P, T, D])
        x_norm = place("x_norm", 152, [P, T, D])
        sq2 = place("sq2", 200, [P, D])
        h2T_hi = place("h2T_hi", 88, [P, KD, S], F32R)
        h2T_lo = place("h2T_lo", 120, [P, KD, S], F32R)
        uT_hi = place("uT_hi", 8, [P, GROUP, S], F32R)
        uT_lo = place("uT_lo", 24, [P, GROUP, S], F32R)
        relu_t = place("relu_t", 40, [P, S])
        relu_sq = place("relu_sq", 44, [P, S])
        w1_at = [184, 48]
        w1_hi = [place(f"w1_hi{i}", w1_at[i], [P, KD, P], F32R) for i in range(2)]
        w1_lo = [place(f"w1_lo{i}", w1_at[i] + 4, [P, KD, P], F32R) for i in range(2)]
        w2_hi = [place(f"w2_hi{i}", 152 + 8 * i, [P, D], F32R) for i in range(4)]
        w2_lo = [place(f"w2_lo{i}", 156 + 8 * i, [P, D], F32R) for i in range(4)]

        PS = ctx.enter_context(nc.psum_tensor("PS", [P, 8, 512], F32))
        PSF = PS[:, :, :].rearrange("p b n -> p (b n)")

        def pair(b):
            return PSF[:, 512 * b:512 * b + 1024]

        const_in = sem("const_in")
        ident_ready = sem("ident_ready")
        const_ready = sem("const_ready")
        x_landed = [sem(f"x_landed{t}") for t in range(T)]
        x_squared = sem("x_squared")
        x_ms_ready = sem("x_ms_ready")
        x_rstd_ready = sem("x_rstd_ready")
        x_normed = sem("x_normed")
        xT_done = sem("xT_done")
        hT_hi_done = sem("hT_hi_done")
        hT_ready = sem("hT_ready")
        zraw_landed = [sem(f"zraw_landed{i}") for i in range(4)]
        zw_hi_done = sem("zw_hi_done")
        zw_ready = sem("zw_ready")
        z_tile_done = sem("z_tile_done")
        z_evac = sem("z_evac")
        graw_landed = [sem(f"graw_landed{i}") for i in range(2)]
        gw_hi_done = sem("gw_hi_done")
        gw_ready = sem("gw_ready")
        gate_done = sem("gate_done")
        gate_ready = sem("gate_ready")
        z_squared = sem("z_squared")
        z_summed = sem("z_summed")
        z_ms_ready = sem("z_ms_ready")
        z_rstd_ready = sem("z_rstd_ready")
        z_normed = sem("z_normed")
        angle_ready = sem("angle_ready")
        rope_ready = sem("rope_ready")
        aT_done = sem("aT_done")
        aT_ready = sem("aT_ready")
        ka_pad_ready = sem("ka_pad_ready")
        pos_landed = sem("pos_landed")
        pos_ready = sem("pos_ready")
        dist_abs = sem("dist_abs")
        dist_ready = sem("dist_ready")
        v_odd_ready = sem("v_odd_ready")
        a_qk_done = sem("a_qk_done")
        a_sc_ready = sem("a_sc_ready")
        a_exp_done = sem("a_exp_done")
        a_ptf_done = sem("a_ptf_done")
        a_pth_done = sem("a_pth_done")
        a_ptf_ready = sem("a_ptf_ready")
        a_pth_ready = sem("a_pth_ready")
        a_pv_done = sem("a_pv_done")
        a_y_ready = sem("a_y_ready")
        wuq_landed = sem("wuq_landed")
        b_proj_done = sem("b_proj_done")
        b_nat_ready = sem("b_nat_ready")
        b_v_ready = sem("b_v_ready")
        b_squared = sem("b_squared")
        b_summed = sem("b_summed")
        b_ms_ready = sem("b_ms_ready")
        b_rstd_ready = sem("b_rstd_ready")
        b_normed = sem("b_normed")
        bT_done = sem("bT_done")
        qbT_ready = sem("qbT_ready")
        kbT_ready = sem("kbT_ready")
        b_qk_done = sem("b_qk_done")
        b_max_ready = sem("b_max_ready")
        b_exp_done = sem("b_exp_done")
        b_pt0_done = sem("b_pt0_done")
        b_pt1_done = sem("b_pt1_done")
        b_pt0_ready = sem("b_pt0_ready")
        b_pt1_ready = sem("b_pt1_ready")
        b_pv_done = sem("b_pv_done")
        b_y_ready = sem("b_y_ready")
        yT_done = sem("yT_done")
        yT_hi_done = sem("yT_hi_done")
        yT_ready = sem("yT_ready")
        raw_landed = [sem(f"raw_landed{i}") for i in range(2)]
        bw_hi_done = sem("bw_hi_done")
        bw_ready = sem("bw_ready")
        branch_done = sem("branch_done")
        merged_ready = sem("merged_ready")
        mT_hi_done = sem("mT_hi_done")
        mT_ready = sem("mT_ready")
        ow_hi_done = sem("ow_hi_done")
        ow_ready = sem("ow_ready")
        xr_landed = [sem(f"xr_landed{t}") for t in range(T)]
        o_done = sem("o_done")
        xr_added = sem("xr_added")
        x2_squared = sem("x2_squared")
        x2_ms_ready = sem("x2_ms_ready")
        x2_rstd_ready = sem("x2_rstd_ready")
        x2_normed = sem("x2_normed")
        x2T_done = sem("x2T_done")
        h2T_hi_done = sem("h2T_hi_done")
        h2T_ready = sem("h2T_ready")
        w1_hi_done = sem("w1_hi_done")
        w1_ready = sem("w1_ready")
        w2_hi_done = sem("w2_hi_done")
        w2_ready = sem("w2_ready")
        up_done = sem("up_done")
        relu_ready = sem("relu_ready")
        relu_sq_ready = sem("relu_sq_ready")
        uT_hi_done = sem("uT_hi_done")
        uT_ready = sem("uT_ready")
        down_done = sem("down_done")
        x3_added = sem("x3_added")
        out_written = sem("out_written")
        dve_step = sem("dve_step")
        gated_step = sem("gated_step")

        steps = [0]

        def link(dve, instruction):
            steps[0] += 1
            instruction.then_inc(dve_step, 1)
            dve.wait_ge(dve_step, steps[0])

        def bcast(ap, shape):
            return ap.to_broadcast(shape)

        def peeled(eng, n, body):
            body(0, True)
            with eng.Fori(1, n) as i:
                body(i, False)

        def unrolled(n, body):
            for i in range(n):
                body(i, i == 0)

        n_const = [0]

        block = ctx.enter_context(nc.Block())

        @block.sync
        def _(sp):
            for t in range(T):
                sp.dma_start(x_in[:, t, :], x_d[t]).then_inc(x_landed[t], 16)
            for n in range(2 * Z_CHUNKS):
                c, kh = n // 2, n % 2
                if n >= 4:
                    sp.wait_ge(zw_ready, n - 3)
                sp.dma_start(z_raw[n % 4][:, :, :],
                             w_in_d[kh * 512:(kh + 1) * 512, c * ZC:(c + 1) * ZC].rearrange("(k p) n -> p k n", p=P)
                             ).then_inc(zraw_landed[n % 4], 16)
            sp.wait_ge(zw_ready, 2 * Z_CHUNKS)

            def gate_loads(i, first):
                for s in range(2):
                    if not first:
                        sp.wait_ge(gw_ready, 2 * i + s - 1)
                    sp.dma_start(g_raw[s][:, :, :],
                                 w_in_d[:, bass.ds(Z_COLS + (2 * i + s) * P, P)].rearrange("(k p) n -> p k n", p=P)
                                 ).then_inc(graw_landed[s], 16)
            peeled(sp, KD, gate_loads)

            sp.wait_ge(gate_done, 2 * KD)
            sp.dma_start(pos_row_i[:, :], positions[0:1, :].partition_broadcast(P)).then_inc(pos_landed, 16)
            sp.dma_start(wuq[:, :, :], w_uq_d[:, 0:B_GROUP * QK].rearrange("(k p) n -> p k n", p=P)
                         ).then_inc(wuq_landed, 16)
            sp.dma_start(wukv[:, :], w_ukv_d[:, 0:B_GROUP * P]).then_inc(wuq_landed, 16)
            sp.wait_ge(b_proj_done, 2 * T)
            sp.dma_start(wuq[:, :, :], w_uq_d[:, B_GROUP * QK:2 * B_GROUP * QK].rearrange("(k p) n -> p k n", p=P)
                         ).then_inc(wuq_landed, 16)
            sp.dma_start(wukv[:, :], w_ukv_d[:, B_GROUP * P:2 * B_GROUP * P]).then_inc(wuq_landed, 16)

            sp.wait_ge(bT_done, 4 * 8)

            def branch_loads(i, first):
                for s in range(2):
                    if not first:
                        sp.wait_ge(bw_ready, 2 * i + s - 1)
                    dst = raw[s][:, :].rearrange("p (k n) -> p k n", n=P)
                    cols = bass.ds((2 * i + s) * P, P)
                    sp.dma_start(dst[:, 0:4, :], w_branch_a[0][:, cols].rearrange("(k p) n -> p k n", p=P)
                                 ).then_inc(raw_landed[s], 16)
                    sp.dma_start(dst[:, 4:8, :], w_branch_b[0][:, cols].rearrange("(k p) n -> p k n", p=P)
                                 ).then_inc(raw_landed[s], 16)
            peeled(sp, KD // 2, branch_loads)

            def out_load(k):
                if k < 2:
                    sp.wait_ge(bw_ready, KD - 1 + k)
                else:
                    sp.wait_ge(ow_ready, k - 1)
                sp.dma_start(raw[k % 2][:, :], w_out_d[k * P:(k + 1) * P, :]).then_inc(raw_landed[k % 2], 16)

            for k in range(4):
                out_load(k)
            sp.wait_ge(branch_done, 2 * KD)
            for t in range(T):
                sp.dma_start(xr[:, t, :], x_d[t]).then_inc(xr_landed[t], 16)
            for k in range(4, 8):
                out_load(k)

            def ff_loads(g, first):
                def load(n, what, j, *split):
                    for s_, v in split:
                        sp.wait_ge(s_, v)
                    if what == 1:
                        src = w1_d[:, bass.ds(g * (GROUP * P) + j * P, P)].rearrange("(k p) n -> p k n", p=P)
                        dst = raw[n % 2][:, :].rearrange("p (k n) -> p k n", n=P)
                    else:
                        src = w2_d[bass.ds(g * (GROUP * P) + j * P, P), :]
                        dst = raw[n % 2][:, :]
                    sp.dma_start(dst, src).then_inc(raw_landed[n % 2], 16)
                load(0, 1, 0, (ow_ready, 7) if first else (w1_ready, 4 * g))
                load(1, 1, 1, (ow_ready, 8) if first else (w2_ready, 4 * g))
                load(2, 2, 0, (w1_ready, 4 * g + 1))
                load(3, 2, 1, (w1_ready, 4 * g + 2))
                load(4, 1, 2, (w2_ready, 4 * g + 1))
                load(5, 2, 2, (w2_ready, 4 * g + 2))
                load(6, 1, 3, (w1_ready, 4 * g + 3))
                load(7, 2, 3, (w2_ready, 4 * g + 3))
            peeled(sp, FF_GROUPS, ff_loads)
            for t in range(T):
                sp.wait_ge(x3_added, T * (FF_GROUPS - 1) + t + 1)
                sp.dma_start(out_d[t], xr[:, t, :]).then_inc(out_written, 16)
            sp.wait_ge(out_written, 16 * T)

        @block.gpsimd
        def _(pool):
            pool.memset(ident[:, :], 0.0).then_inc(ident_ready, 1)
            pool.memset(minus_half[:, :], -0.5).then_inc(const_ready, 1)
            for i in range(RH):
                pool.memset(inv_f[:, i:i + 1], INV_FREQ[i]).then_inc(const_ready, 1)
            pool.wait_ge(ident_ready, 1)
            pool.affine_select(out=ident[:, :], in_=ident[:, :], compare_op=ALU.not_equal, fill=1.0, base=0,
                               pattern=[[-1, P]], channel_multiplier=1).then_inc(ident_ready, 1)

            def split(raw_ap, hi_ap, lo_ap, hi_done, count, ready):
                pool.tensor_scalar(hi_ap, raw_ap, 1.0, 1.0, ALU.mult, ALU.mult).then_inc(hi_done, 1)
                pool.wait_ge(hi_done, count)
                pool.tensor_tensor(lo_ap, raw_ap, hi_ap, ALU.subtract).then_inc(ready, 1)

            def power(out_ap, in_ap, n, shape):
                e = minus_half[:, 0:n]
                if len(shape) == 3:
                    e = e.rearrange("p (a b) -> p a b", b=shape[2])
                return pool.tensor_tensor(out_ap, in_ap, e, ALU.pow)

            def z_split(n):
                c, kh = n // 2, n % 2
                pool.wait_ge(zraw_landed[n % 4], 16 * (n // 4 + 1))
                if c >= 2:
                    pool.wait_ge(z_tile_done, T * (c - 1))
                split(z_raw[n % 4][:, :, :], zw_hi[c % 2][:, 4 * kh:4 * kh + 4, :],
                      zw_lo[c % 2][:, 4 * kh:4 * kh + 4, :], zw_hi_done, n + 1, zw_ready)

            pool.wait_ge(const_ready, 1 + RH)
            for h in range(2):
                pool.wait_ge(x_ms_ready, h + 1)
                power(x_rstd[:, 4 * h:4 * h + 4], x_ms[:, 4 * h:4 * h + 4], 4, (P, 4)).then_inc(x_rstd_ready, 1)
                z_split(h)
            for n in range(2, 2 * Z_CHUNKS):
                z_split(n)

            pool.wait_ge(hT_ready, 2 * KD)

            def gate_splits(base):
                def body(i, first):
                    for s in range(2):
                        u = 2 * i + s + base
                        pool.wait_ge(graw_landed[s], 16 * (i + 1) + 8 * base)
                        if not (first and base == 0):
                            pool.wait_ge(gate_done, u - 1)
                        split(g_raw[s][:, :, :], gw_hi[s][:, :, :], gw_lo[s][:, :, :], gw_hi_done, u + 1, gw_ready)
                return body
            unrolled(KD // 2, gate_splits(0))
            pool.wait_ge(z_ms_ready, 4)
            power(z_rstd[:, :, :], z_ms[:, :, :], T * N_STAT, (P, T, N_STAT)).then_inc(z_rstd_ready, 1)
            unrolled(KD // 2, gate_splits(KD))

            pool.wait_ge(gate_done, 2 * KD)
            pool.memset(kaT[:, :, 0:CHUNK], 0.0).then_inc(ka_pad_ready, 1)
            pool.memset(pos_row[:, 0:CHUNK], 0.0).then_inc(ka_pad_ready, 1)

            for n in range(2 * B_GROUPS):
                pool.wait_ge(b_ms_ready, 2 * (n + 1))
                power(b_rstd[:, :, :], b_ms[:, :, :], 4 * 2 * B_GROUP, (P, 4, 2 * B_GROUP)).then_inc(b_rstd_ready, 1)

            def branch_splits(i, first):
                for s in range(2):
                    d = 2 * i + s
                    pool.wait_ge(raw_landed[s], 32 * (i + 1))
                    if first and s == 1:
                        pool.wait_ge(b_pv_done, B_GROUPS * B_GROUP * T)
                    if not first:
                        pool.wait_ge(branch_done, 2 * (d - 1))
                    split(raw[s][:, :].rearrange("p (k n) -> p k n", n=P), bw_hi[s][:, :, :], bw_lo[s][:, :, :],
                          bw_hi_done, d + 1, bw_ready)
            unrolled(KD // 2, branch_splits)

            for k in range(8):
                pool.wait_ge(raw_landed[k % 2], 32 * 4 + 16 * (k // 2 + 1))
                if k == 0:
                    pool.wait_ge(yT_done, 16)
                if k == 4:
                    pool.wait_ge(branch_done, 2 * KD)
                split(raw[k % 2][:, :], ow_hi[k][:, :], ow_lo[k][:, :], ow_hi_done, k + 1, ow_ready)

            def ff_splits(g, first):
                landed = 32 * 4 + 16 * 4 + 64 * g

                def unit(n, what, j):
                    pool.wait_ge(raw_landed[n % 2], landed + 16 * (n // 2 + 1))
                    if what == 1:
                        if first and j < 2:
                            if j == 1:
                                pool.wait_ge(o_done, 2 * T)
                        else:
                            pool.wait_ge(up_done, 4 * g + j - 1)
                        split(raw[n % 2][:, :].rearrange("p (k n) -> p k n", n=P), w1_hi[j % 2][:, :, :],
                              w1_lo[j % 2][:, :, :], w1_hi_done, 4 * g + j + 1, w1_ready)
                    else:
                        if j == 0:
                            if first:
                                pool.wait_ge(x2T_done, 2 * KD)
                            else:
                                pool.wait_ge(down_done, T * g)
                        split(raw[n % 2][:, :], w2_hi[j][:, :], w2_lo[j][:, :], w2_hi_done, 4 * g + j + 1, w2_ready)
                unit(0, 1, 0)
                if first:
                    for h in range(2):
                        pool.wait_ge(x2_ms_ready, h + 1)
                        power(x_rstd[:, 4 * h:4 * h + 4], x_ms[:, 4 * h:4 * h + 4], 4, (P, 4)
                              ).then_inc(x2_rstd_ready, 1)
                unit(1, 1, 1)
                unit(2, 2, 0)
                unit(3, 2, 1)
                unit(4, 1, 2)
                unit(5, 2, 2)
                unit(6, 1, 3)
                unit(7, 2, 3)
            unrolled(FF_GROUPS, ff_splits)

        @block.scalar
        def _(act):
            def load(dst, src):
                act.dma_start(dst, src).then_inc(const_in, 16)
                n_const[0] += 1

            def column(v, a, b):
                return v[0, a:b].rearrange("(p o) -> p o", o=1)

            with nc.allow_non_contiguous_dma(reason="gains and biases, a few KiB in all"):
                load(g_mix_c[:, :], g_mix[0].rearrange("(j p) -> p j", p=P))
                load(pos_i[:, :], positions[0].rearrange("(t p) -> p t", p=P))
                load(b_gate_c[:, :], b_gate[0].rearrange("(j p) -> p j", p=P))
                load(g_mlp_c[:, :], g_mlp[0].rearrange("(j p) -> p j", p=P))
                load(g_cq_c[:, :], g_cq[0].rearrange("(j p) -> p j", p=P))
                load(g_ckv_c[:, :], column(g_ckv, 0, KV_RANK))
                for r in (0, A_DIM):
                    load(g_qa_c[r:r + A_DIM, :], column(g_qa, 0, A_DIM))
                    load(g_ka_c[r:r + A_DIM, :], column(g_ka, 0, A_DIM))
                load(g_qb_c[0:NOPE, :], column(g_qb, 0, NOPE))
                load(g_kb_c[0:NOPE, :], column(g_kb, 0, NOPE))
                load(g_qr[:, :], g_qb[0:1, NOPE:QK].partition_broadcast(P))
                load(g_kr[:, :], g_kb[0:1, NOPE:QK].partition_broadcast(P))
                load(sink_r[:, :], sinks_a[0:1, :].partition_broadcast(P))

            act.wait_ge(angle_ready, 2)
            act.activation(sin_t[:, :, :], rope_tmp[4][:, :, :], ACT.Sin).then_inc(rope_ready, 1)
            act.activation(cos_t[:, :, :], rope_tmp[5][:, :, :], ACT.Sin).then_inc(rope_ready, 1)

            for t in range(T):
                act.wait_ge(x_landed[t], 16)
                if t >= 1:
                    act.wait_ge(x_squared, t)
                act.activation(sq[:, 0:D], x_in[:, t, :], ACT.Square, accum_out=x_ss[:, t:t + 1]
                               ).then_inc(x_squared, 1)
            for n in range(2 * KD):
                h, j = n // KD, n % KD
                act.wait_ge(xT_done, n + 1)
                act.activation(hT_hi[:, j, h * HALF:(h + 1) * HALF], PS[:, n % 8, :], ACT.Copy,
                               scale=g_mix_c[:, j:j + 1]).then_inc(hT_hi_done, 1)

            for n in range(Z_CHUNKS * T):
                c, t = n // T, n % T
                act.wait_ge(z_tile_done, n + 1)
                act.activation(Z[:, t, c * ZC:(c + 1) * ZC], PS[:, t, 0:ZC], ACT.Copy).then_inc(z_evac, 1)

            act.wait_ge(z_evac, Z_CHUNKS * T)

            def gate_a(i, first):
                for s in range(2):
                    u = 2 * i + s
                    act.wait_ge(gate_done, u + 1)
                    act.activation(gate[:, u, :], pair(2 * s), ACT.Sigmoid, bias=b_gate_c[:, bass.ds(u, 1)]
                                   ).then_inc(gate_ready, 1)
                    if not (first and s == 0):
                        act.wait_ge(z_summed, 4 * u)
                    act.activation(sq[:, :], Z[:, u, :], ACT.Square).then_inc(z_squared, 1)

            def gate_b(i, first):
                for s in range(2):
                    u = 2 * i + s + KD
                    act.wait_ge(gate_done, u + 1)
                    act.activation(gate[:, u, :], pair(2 * s), ACT.Sigmoid, bias=b_gate_c[:, bass.ds(u, 1)]
                                   ).then_inc(gate_ready, 1)
            peeled(act, KD // 2, gate_a)
            with act.Fori(0, KD // 2) as i:
                gate_b(i, False)

            act.wait_ge(ka_pad_ready, 2)
            n = 0
            for h in range(2):
                cols = slice(h * HALF, (h + 1) * HALF)
                for p in range(4):
                    act.wait_ge(aT_done, n + 1)
                    act.activation(qaT[:, p, cols], PS[:, n % 8, :], ACT.Copy, scale=gqk_a[:, 0:1]).then_inc(aT_ready, 1)
                    n += 1
                for v in range(A_KV):
                    act.wait_ge(aT_done, n + 1)
                    act.activation(kaT[:, v, CHUNK + h * HALF:CHUNK + (h + 1) * HALF], PS[:, n % 8, :], ACT.Copy
                                   ).then_inc(aT_ready, 1)
                    n += 1
            act.wait_ge(pos_ready, 1)
            for t in range(T):
                act.activation(dist[:, t, :], pos_row[:, t * P:t * P + WIN], ACT.Abs, scale=-1.0,
                               bias=pos_c[:, t:t + 1]).then_inc(dist_abs, 1)
            act.activation(v_odd[0:CHUNK, :, :], Z[CHUNK:P, :, C_V:C_V + A_KV * A_DIM], ACT.Copy
                           ).then_inc(v_odd_ready, 1)
            for h in range(2):
                cols = slice(h * HALF, (h + 1) * HALF)
                for j in range(2):
                    act.wait_ge(aT_done, n + 1)
                    act.activation(cqT[:, j, cols], PS[:, n % 8, :], ACT.Copy, scale=g_cq_c[:, j:j + 1]
                                   ).then_inc(aT_ready, 1)
                    n += 1
                act.wait_ge(aT_done, n + 1)
                act.activation(ckvT[:, cols], PS[:, n % 8, :], ACT.Copy, scale=g_ckv_c[:, 0:1]).then_inc(aT_ready, 1)
                n += 1

            def a_exp(u):
                s = u % 2
                act.wait_ge(a_sc_ready, u + 1)
                if u >= 2:
                    act.wait_ge(a_y_ready, u - 1)
                for g in range(A_GROUP):
                    act.activation(scA[:, s, g, 0:WIN + 1], scA[:, s, g, 0:WIN + 1], ACT.Exp,
                                   bias=a_nmax[:, s, g:g + 1], accum_out=a_sum[:, s, g:g + 1]).then_inc(a_exp_done, 1)

            def a_ptf(u):
                act.wait_ge(a_ptf_done, u + 1)
                if u >= 2:
                    act.wait_ge(a_pv_done, u - 1)
                act.activation(ptA_full[u % 2][:, :, :].rearrange("p g q -> p (g q)"), PS[:, 4, :], ACT.Copy
                               ).then_inc(a_ptf_ready, 1)
            for u in range(2 * T + 1):
                if u < 2 * T:
                    a_exp(u)
                if u >= 1:
                    a_ptf(u - 1)

            w0 = 0
            for g in range(B_GROUPS):
                for n in range(T):
                    hh, i = n // 4, n % 4
                    m = g * T + n
                    act.wait_ge(b_proj_done, 2 * m + 2)
                    if n == 0 and g:
                        act.wait_ge(b_pv_done, w0)
                    if n == 0 and not g:
                        act.wait_ge(a_y_ready, 2 * T)
                    qb, kb = PS[:, 2 * i, 0:B_GROUP * QK], PS[:, 2 * i + 1, :].rearrange("p (h c) -> p h c", c=P)
                    act.activation(q_nat[hh][:, i, :, :].rearrange("p h c -> p (h c)"), qb, ACT.Copy
                                   ).then_inc(b_nat_ready, 1)
                    act.activation(k_nat[hh][:, i, :, 0:NOPE], kb[:, :, 0:NOPE], ACT.Copy).then_inc(b_nat_ready, 1)
                    if m:
                        act.wait_ge(b_summed, 2 * m)
                    act.activation(sqB[:, 0:B_GROUP * QK], qb, ACT.Square).then_inc(b_squared, 1)
                    act.activation(sqB[:, B_GROUP * QK:].rearrange("p (h c) -> p h c", c=NOPE), kb[:, :, 0:NOPE],
                                   ACT.Square).then_inc(b_squared, 1)
                for n in range(16):
                    m = 16 * g + n
                    hh, what, h = n // 8, (n % 8) // 4, n % 4
                    if what == 0:
                        act.wait_ge(bT_done, m + 1)
                        act.activation(qbT[0:QK, h, hh * HALF:(hh + 1) * HALF], PS[0:QK, n % 8, :], ACT.Copy,
                                       scale=gqk_b[0:QK, 0:1]).then_inc(qbT_ready, 1)

                def b_exp(w):
                    s, i = w % 2, w % T
                    act.wait_ge(b_max_ready, w + 1)
                    if w >= 2:
                        act.wait_ge(b_y_ready, w - 1)
                    act.activation(prB[s][:, 0:(i + 1) * P], pair(2 * s)[:, 0:(i + 1) * P], ACT.Exp,
                                   bias=b_nmax[:, s:s + 1], accum_out=b_sum[:, s:s + 1]).then_inc(b_exp_done, 1)

                def b_pt0(w):
                    i = w % T
                    act.wait_ge(b_pt0_done, w + 1)
                    if w >= 2:
                        act.wait_ge(b_pv_done, w - 1)
                    m = min(i + 1, 4)
                    act.activation(ptB[w % 2][:, 0:m, :].rearrange("p k q -> p (k q)"), PS[:, 4, 0:m * P], ACT.Copy
                                   ).then_inc(b_pt0_ready, 1)
                n_w = B_GROUP * T
                for k in range(n_w + 1):
                    if k < n_w:
                        b_exp(w0 + k)
                    if k >= 1:
                        b_pt0(w0 + k - 1)
                w0 += n_w

            act.wait_ge(b_pv_done, w0)
            for n in range(16):
                h, j = n // 8, n % 8
                act.wait_ge(yT_done, n + 1)
                act.activation(yT_hi[:, j, h * HALF:(h + 1) * HALF], PS[:, n % 8, :], ACT.Copy).then_inc(yT_hi_done, 1)

            with act.Fori(0, KD) as d:
                act.wait_ge(merged_ready, d + 1)
                act.activation(mT_hi[:, d, :], merged[:, :], ACT.Copy).then_inc(mT_hi_done, 1)

            for t in range(T):
                act.wait_ge(xr_added, T + t + 1)
                if t:
                    act.wait_ge(x2_squared, t)
                act.activation(sq2[:, :], xr[:, t, :], ACT.Square, accum_out=x_ss[:, t:t + 1]).then_inc(x2_squared, 1)
            for n in range(2 * KD):
                h, j = n // KD, n % KD
                act.wait_ge(x2T_done, n + 1)
                act.activation(h2T_hi[:, j, h * HALF:(h + 1) * HALF], PS[:, n % 8, :], ACT.Copy,
                               scale=g_mlp_c[:, j:j + 1]).then_inc(h2T_hi_done, 1)

            def ff_up(g, first):
                for j in range(GROUP):
                    act.wait_ge(up_done, 4 * g + j + 1)
                    for h in range(2):
                        cols = slice(h * HALF, (h + 1) * HALF)
                        if not (first and j == 0):
                            act.wait_ge(relu_sq_ready, 8 * g + 2 * j - 1 + h)
                        act.activation(relu_t[:, cols], PS[:, 2 * (j % 2) + h, :], ACT.Relu).then_inc(relu_ready, 1)
                    for h in range(2):
                        cols = slice(h * HALF, (h + 1) * HALF)
                        act.wait_ge(relu_sq_ready, 8 * g + 2 * j + h + 1)
                        if j == 0 and h == 0:
                            if first:
                                act.wait_ge(x2T_done, 2 * KD)
                                act.wait_ge(o_done, 2 * T)
                            else:
                                act.wait_ge(down_done, T * g)
                        act.activation(uT_hi[:, j, cols], relu_sq[:, cols], ACT.Copy).then_inc(uT_hi_done, 1)
            peeled(act, FF_GROUPS, ff_up)

        @block.tensor
        def _(pe):
            def split_products(w_hi, w_lo, x_hi, x_lo, outs, k, first, last):
                passes = ((w_hi, x_hi), (w_hi, x_lo), (w_lo, x_hi))
                ins = None
                for n, (st, mv) in enumerate(passes):
                    for o, cut in outs:
                        ins = pe.matmul(o, st, cut(mv), start=first and n == 0, stop=last and n == 2)
                return ins

            def transpose_tiles(bank, tiles, rows=P):
                ins = None
                for i, ap in enumerate(tiles):
                    ins = pe.transpose(PS[0:rows, bank, i * P:(i + 1) * P], ap, ident[:, :])
                return ins

            pe.wait_ge(ident_ready, 2)
            for n in range(2 * KD):
                h, j = n // KD, n % KD
                if j == 0:
                    pe.wait_ge(x_normed, 4 * (h + 1))
                if n >= 8:
                    pe.wait_ge(hT_ready, n - 7)
                transpose_tiles(n % 8, [x_in[:, 4 * h + i, j * P:(j + 1) * P] for i in range(4)]).then_inc(xT_done, 1)

            pe.wait_ge(hT_ready, 2 * KD)
            for c in range(Z_CHUNKS):
                for t in range(T):
                    if c:
                        pe.wait_ge(z_evac, T * (c - 1) + t + 1)
                    rows = slice(t * P, (t + 1) * P)
                    for k in range(KD):
                        if t == 0 and k % 4 == 0:
                            pe.wait_ge(zw_ready, 2 * c + k // 4 + 1)
                        ins = split_products(hT_hi[:, k, rows], hT_lo[:, k, rows], zw_hi[c % 2][:, k, :],
                                             zw_lo[c % 2][:, k, :], [(PS[:, t, 0:ZC], lambda m: m)],
                                             k, k == 0, k == KD - 1)
                    ins.then_inc(z_tile_done, 1)

            halves = [lambda m: m[:, 0:HALF], lambda m: m[:, HALF:S]]

            pe.wait_ge(z_evac, Z_CHUNKS * T)

            def gates(i, first):
                for s in range(2):
                    u = 2 * i + s
                    pe.wait_ge(gw_ready, u + 1)
                    if not first:
                        pe.wait_ge(gate_ready, u - 1)
                    for k in range(KD):
                        ins = split_products(gw_hi[s][:, k, :], gw_lo[s][:, k, :], hT_hi[:, k, :], hT_lo[:, k, :],
                                             [(PS[:, 2 * s + h, :], halves[h]) for h in range(2)],
                                             k, k == 0, k == KD - 1)
                    ins.then_inc(gate_done, 1)
            peeled(pe, KD, gates)

            pe.wait_ge(gate_ready, 2 * KD)
            pe.wait_ge(z_normed, 5 * T)
            n = 0

            def small_transpose(tiles):
                nonlocal n
                if n >= 8:
                    pe.wait_ge(aT_ready, n - 7)
                transpose_tiles(n % 8, tiles).then_inc(aT_done, 1)
                n += 1
            for h in range(2):
                ts = range(4 * h, 4 * h + 4)
                for p in range(4):
                    small_transpose([Z[:, t, p * P:(p + 1) * P] for t in ts])
                for v in range(A_KV):
                    small_transpose([k_dup[:, t, v, :, :].rearrange("p a b -> p (a b)") for t in ts])
            for h in range(2):
                ts = range(4 * h, 4 * h + 4)
                for j in range(2):
                    small_transpose([Z[:, t, C_CQ + j * P:C_CQ + (j + 1) * P] for t in ts])
                small_transpose([Z[:, t, C_CKV:C_CKV + P] for t in ts])
            pe.wait_ge(aT_ready, n)

            def a_qk(u):
                t, v, s = u // 2, u % 2, u % 2
                if u >= 2:
                    pe.wait_ge(a_sc_ready, u - 1)
                for g in range(A_GROUP):
                    head = A_GROUP * v + g
                    r = A_DIM * (head % 2)
                    ins = pe.matmul(PS[:, 2 * s + g % 2, 256 * (g // 2):256 * (g // 2) + WIN],
                                    qaT[r:r + A_DIM, head // 2, t * P:(t + 1) * P],
                                    kaT[r:r + A_DIM, v, t * P:t * P + WIN], start=True, stop=True)
                ins.then_inc(a_qk_done, 1)

            def a_pt(u):
                t, s = u // 2, u % 2
                pe.wait_ge(a_exp_done, A_GROUP * (u + 1))
                if u >= 1:
                    pe.wait_ge(a_ptf_ready, u)
                for g in range(A_GROUP):
                    ins = pe.transpose(PS[:, 4, g * P:(g + 1) * P], scA[:, s, g, CHUNK:WIN], ident[:, :])
                ins.then_inc(a_ptf_done, 1)
                if t:
                    if u >= 3:
                        pe.wait_ge(a_pth_ready, u - 2)
                    for g in range(A_GROUP):
                        ins = pe.transpose(PS[0:CHUNK, 5, g * P:(g + 1) * P], scA[:, s, g, 0:CHUNK], ident[:, :])
                    ins.then_inc(a_pth_done, 1)

            def a_pv(u):
                t, v, s = u // 2, u % 2, u % 2
                pe.wait_ge(a_ptf_ready, u + 1)
                if t:
                    pe.wait_ge(a_pth_ready, u - 1)
                if u >= 2:
                    pe.wait_ge(a_y_ready, u - 1)
                if u == 0:
                    pe.wait_ge(v_odd_ready, 1)
                for g in range(A_GROUP):
                    o = PS[:, 6 + s, g * A_DIM:(g + 1) * A_DIM]
                    if t:
                        pe.matmul(o, ptA_half[s][0:CHUNK, g, :], v_odd[0:CHUNK, t - 1, v * A_DIM:(v + 1) * A_DIM],
                                  start=True, stop=False)
                    ins = pe.matmul(o, ptA_full[s][:, g, :], Z[:, t, C_V + v * A_DIM:C_V + (v + 1) * A_DIM],
                                    start=t == 0, stop=True)
                ins.then_inc(a_pv_done, 1)
            for u in range(2 * T + 2):
                if u < 2 * T:
                    a_qk(u)
                if 1 <= u <= 2 * T:
                    a_pt(u - 1)
                if u >= 2:
                    a_pv(u - 2)

            w0 = 0
            pe.wait_ge(a_y_ready, 2 * T)
            for g in range(B_GROUPS):
                pe.wait_ge(wuq_landed, 32 * (g + 1))
                for n in range(T):
                    m, i = g * T + n, n % 4
                    rows = slice(n * P, (n + 1) * P)
                    if n >= 4:
                        pe.wait_ge(b_squared, 2 * (m - 3))
                        pe.wait_ge(b_v_ready, m - 3)
                    for k in range(2):
                        ins = pe.matmul(PS[:, 2 * i, 0:B_GROUP * QK], cqT[:, k, rows], wuq[:, k, :],
                                        start=k == 0, stop=k == 1)
                    ins.then_inc(b_proj_done, 1)
                    pe.matmul(PS[:, 2 * i + 1, :], ckvT[:, rows], wukv[:, :], start=True, stop=True
                              ).then_inc(b_proj_done, 1)
                for n in range(16):
                    m = 16 * g + n
                    hh, what, h = n // 8, (n % 8) // 4, n % 4
                    if n % 8 == 0:
                        pe.wait_ge(b_normed, 2 * g + hh + 1)
                        pe.wait_ge(b_squared, 2 * T * (g + 1))
                        pe.wait_ge(b_v_ready, T * (g + 1))
                    if n >= 8:
                        pe.wait_ge((qbT_ready, kbT_ready)[what], 8 * g + h + 1)
                    src = (q_nat, k_nat)[what][hh]
                    transpose_tiles(n % 8, [src[:, i, h, :] for i in range(4)], QK).then_inc(bT_done, 1)
                pe.wait_ge(qbT_ready, 8 * (g + 1))
                pe.wait_ge(kbT_ready, 8 * (g + 1))

                def b_qk(w):
                    s, h, i = w % 2, (w // T) % B_GROUP, w % T
                    if w - w0 >= 2:
                        pe.wait_ge(b_exp_done, w - 1)
                    for c in range(0, (i + 1) * P, 512):
                        m = min(512, (i + 1) * P - c)
                        ins = pe.matmul(pair(2 * s)[:, c:c + m], qbT[0:QK, h, i * P:(i + 1) * P],
                                        kbT[0:QK, h, c:c + m], start=True, stop=True)
                    ins.then_inc(b_qk_done, 1)

                def b_pt(w):
                    s, i = w % 2, w % T
                    pe.wait_ge(b_exp_done, w + 1)
                    if w >= 1:
                        pe.wait_ge(b_pt0_ready, w)
                    for k in range(min(i + 1, 4)):
                        ins = pe.transpose(PS[:, 4, k * P:(k + 1) * P], prB[s][:, k * P:(k + 1) * P], ident[:, :])
                    ins.then_inc(b_pt0_done, 1)
                    if i >= 4:
                        done = 4 * (w // T) + i - 4
                        if done:
                            pe.wait_ge(b_pt1_ready, done)
                        for k in range(4, i + 1):
                            ins = pe.transpose(PS[:, 5, (k - 4) * P:(k - 3) * P], prB[s][:, k * P:(k + 1) * P],
                                               ident[:, :])
                        ins.then_inc(b_pt1_done, 1)

                def b_pv(w):
                    s, h, i = w % 2, (w // T) % B_GROUP, w % T
                    pe.wait_ge(b_pt0_ready, w + 1)
                    if i >= 4:
                        pe.wait_ge(b_pt1_ready, 4 * (w // T) + i - 3)
                    if w >= 2:
                        pe.wait_ge(b_y_ready, w - 1)
                    for k in range(i + 1):
                        ins = pe.matmul(PS[:, 6 + s, 0:V_DIM], ptB[s][:, k, :], vB[:, k, h, :],
                                        start=k == 0, stop=k == i)
                    ins.then_inc(b_pv_done, 1)
                n_w = B_GROUP * T
                for k in range(n_w + 2):
                    if k < n_w:
                        b_qk(w0 + k)
                    if 1 <= k <= n_w:
                        b_pt(w0 + k - 1)
                    if k >= 2:
                        b_pv(w0 + k - 2)
                w0 += n_w
                pe.wait_ge(b_y_ready, w0)

            for n in range(16):
                h, j = n // 8, n % 8
                if n >= 8:
                    pe.wait_ge(yT_ready, n - 7)
                src, jj = (yA, j) if j < 4 else (yB, j - 4)
                transpose_tiles(n % 8, [src[:, 4 * h + i, jj * P:(jj + 1) * P] for i in range(4)]
                                ).then_inc(yT_done, 1)
            pe.wait_ge(yT_ready, 16)

            def branches(i, first):
                for s in range(2):
                    d = 2 * i + s
                    pe.wait_ge(bw_ready, d + 1)
                    if not first:
                        pe.wait_ge(merged_ready, d - 1)
                    for b in range(2):
                        for k in range(4):
                            kk = 4 * b + k
                            ins = split_products(bw_hi[s][:, kk, :], bw_lo[s][:, kk, :], yT_hi[:, kk, :],
                                                 yT_lo[:, kk, :],
                                                 [(PS[:, 4 * s + 2 * b + h, :], halves[h]) for h in range(2)],
                                                 k, k == 0, k == 3)
                        ins.then_inc(branch_done, 1)
            peeled(pe, KD // 2, branches)

            pe.wait_ge(mT_ready, KD)
            for n in range(2 * T):
                r, t = n // T, n % T
                if n >= 4:
                    pe.wait_ge(xr_added, n - 3)
                rows = slice(t * P, (t + 1) * P)
                for k in range(4 * r, 4 * r + 4):
                    if t == 0:
                        pe.wait_ge(ow_ready, k + 1)
                    ins = split_products(mT_hi[:, k, rows], mT_lo[:, k, rows], ow_hi[k][:, :], ow_lo[k][:, :],
                                         [(PS[:, 2 * (n % 4) + h, :], halves[h]) for h in range(2)],
                                         k, k == 4 * r, k == 4 * r + 3)
                ins.then_inc(o_done, 1)

            pe.wait_ge(xr_added, 2 * T)
            for n in range(2 * KD):
                h, j = n // KD, n % KD
                if j == 0:
                    pe.wait_ge(x2_normed, 4 * (h + 1))
                if n >= 8:
                    pe.wait_ge(h2T_ready, n - 7)
                transpose_tiles(n % 8, [x_norm[:, 4 * h + i, j * P:(j + 1) * P] for i in range(4)]
                                ).then_inc(x2T_done, 1)
            pe.wait_ge(h2T_ready, 2 * KD)

            def ff(g, first):
                for j in range(GROUP):
                    pe.wait_ge(w1_ready, 4 * g + j + 1)
                    if not (first and j < 2):
                        pe.wait_ge(relu_ready, 8 * g + 2 * j - 2)
                    for k in range(KD):
                        ins = split_products(w1_hi[j % 2][:, k, :], w1_lo[j % 2][:, k, :], h2T_hi[:, k, :],
                                             h2T_lo[:, k, :],
                                             [(PS[:, 2 * (j % 2) + h, :], halves[h]) for h in range(2)],
                                             k, k == 0, k == KD - 1)
                    ins.then_inc(up_done, 1)
                for t in range(T):
                    rows = slice(t * P, (t + 1) * P)
                    if not (first and t < 2):
                        pe.wait_ge(x3_added, T * g + t - 1)
                    for j in range(GROUP):
                        if t == 0:
                            pe.wait_ge(w2_ready, 4 * g + j + 1)
                            pe.wait_ge(uT_ready, 8 * g + 2 * j + 1)
                        if t == 4 and j == 0:
                            pe.wait_ge(uT_ready, 8 * g + 8)
                        ins = split_products(uT_hi[:, j, rows], uT_lo[:, j, rows], w2_hi[j][:, :], w2_lo[j][:, :],
                                             [(PS[:, 4 + 2 * (t % 2) + h, :], halves[h]) for h in range(2)],
                                             j, j == 0, j == GROUP - 1)
                    ins.then_inc(down_done, 1)
            peeled(pe, FF_GROUPS, ff)

        @block.vector
        def _(dve):
            dve.wait_ge(const_in, 16 * n_const[0])
            link(dve, dve.memset(gqk_b[:, :], QK ** -0.5))
            link(dve, dve.tensor_copy(pos_c[:, :], pos_i[:, :]))
            link(dve, dve.tensor_tensor(gqk_a[:, :], g_qa_c[:, :], g_ka_c[:, :], ALU.mult))
            link(dve, dve.tensor_scalar(gqk_a[:, :], gqk_a[:, :], A_DIM ** -0.5, None, ALU.mult))
            link(dve, dve.tensor_tensor(g_qb_c[0:NOPE, :], g_qb_c[0:NOPE, :], g_kb_c[0:NOPE, :], ALU.mult))
            link(dve, dve.tensor_tensor(gqk_b[0:NOPE, :], gqk_b[0:NOPE, :], g_qb_c[0:NOPE, :], ALU.mult))
            dve.wait_ge(const_ready, 1 + RH)
            ang, turns, part, _r, s_ang, c_ang = [r[:, :, :] for r in rope_tmp]
            full = [P, T, RH]
            link(dve, dve.tensor_tensor(ang, bcast(pos_c[:, :].rearrange("p (t o) -> p t o", o=1), full),
                                        bcast(inv_f[:, :].rearrange("p (o f) -> p o f", o=1), full), ALU.mult))
            for red, quarter in ((s_ang, 0.0), (c_ang, 0.25)):
                link(dve, dve.tensor_scalar(turns, ang, 1.0 / TWO_PI, quarter, ALU.mult, ALU.add))
                link(dve, dve.tensor_scalar(turns, turns, ROUND, ROUND, ALU.add, ALU.subtract))
                link(dve, dve.tensor_scalar(part, turns, PI_A, None, ALU.mult))
                link(dve, dve.tensor_tensor(red, ang, part, ALU.subtract))
                link(dve, dve.tensor_scalar(part, turns, PI_B, None, ALU.mult))
                link(dve, dve.tensor_tensor(red, red, part, ALU.subtract))
                link(dve, dve.tensor_scalar(part, turns, PI_C, None, ALU.mult))
                link(dve, dve.tensor_tensor(red, red, part, ALU.subtract))
                if quarter:
                    link(dve, dve.tensor_scalar(red, red, TWO_PI * quarter, None, ALU.add))
                dve.tensor_scalar(red, red, SIN_MAX, -SIN_MAX, ALU.min, ALU.max).then_inc(angle_ready, 1)

            for h in range(2):
                ts = slice(4 * h, 4 * h + 4)
                dve.wait_ge(x_squared, 4 * (h + 1))
                dve.tensor_scalar(x_ms[:, ts], x_ss[:, ts], 1.0 / D, EPS, ALU.mult, ALU.add).then_inc(x_ms_ready, 1)
            for t in range(T):
                if t % 4 == 0:
                    dve.wait_ge(x_rstd_ready, t // 4 + 1)
                dve.tensor_scalar(x_in[:, t, :], x_in[:, t, :], x_rstd[:, t:t + 1], None, ALU.mult
                                  ).then_inc(x_normed, 1)
            for n in range(2 * KD):
                h, j = n // KD, n % KD
                cols = slice(h * HALF, (h + 1) * HALF)
                dve.wait_ge(hT_hi_done, n + 1)
                dve.scalar_tensor_tensor(out=hT_lo[:, j, cols], in0=PS[:, n % 8, :], scalar=g_mix_c[:, j:j + 1],
                                         in1=hT_hi[:, j, cols], op0=ALU.mult, op1=ALU.subtract).then_inc(hT_ready, 1)

            def z_sums(i, first):
                for s in range(2):
                    t = 2 * i + s
                    dve.wait_ge(z_squared, t + 1)
                    dve.tensor_reduce(z_ss[:, t, 0:10], sq[:, 0:C_V].rearrange("p (h c) -> p h c", c=A_DIM), AX.X,
                                      ALU.add).then_inc(z_summed, 1)
                    for st, a, b in ((ST_CQ, C_CQ, C_CKV), (ST_CKV, C_CKV, C_KR), (ST_KR, C_KR, Z_COLS)):
                        dve.tensor_reduce(z_ss[:, t, st:st + 1], sq[:, a:b], AX.X, ALU.add).then_inc(z_summed, 1)
            with dve.Fori(0, T // 2) as i:
                z_sums(i, False)
            dve.wait_ge(z_summed, 4 * T)
            dve.wait_ge(dve_step, steps[0])
            for a, b, width in ((0, 10, A_DIM), (ST_CQ, ST_CQ + 1, Q_RANK), (ST_CKV, ST_CKV + 1, KV_RANK),
                                (ST_KR, ST_KR + 1, ROPE)):
                dve.tensor_scalar(z_ms[:, :, a:b], z_ss[:, :, a:b], 1.0 / width, EPS, ALU.mult, ALU.add
                                  ).then_inc(z_ms_ready, 1)
            dve.wait_ge(z_rstd_ready, 1)

            def z_norms(i, first):
                for s in range(2):
                    t = 2 * i + s
                    q = Z[:, t, 0:C_K].rearrange("p (h c) -> p h c", c=A_DIM)
                    k = Z[:, t, C_K:C_V].rearrange("p (h c) -> p h c", c=A_DIM)
                    r = z_rstd[:, t, :].rearrange("p (n o) -> p n o", o=1)
                    dve.tensor_tensor(q, q, bcast(r[:, 0:A_HEADS, :], [P, A_HEADS, A_DIM]), ALU.mult
                                      ).then_inc(z_normed, 1)
                    for c in range(2):
                        dve.tensor_tensor(k_dup[:, t, :, c, :], k, bcast(r[:, A_HEADS:ST_CQ, :], [P, A_KV, A_DIM]),
                                          ALU.mult).then_inc(z_normed, 1)
                    for st, a, b in ((ST_CQ, C_CQ, C_CKV), (ST_CKV, C_CKV, C_KR)):
                        v = Z[:, t, a:b].rearrange("p (o c) -> p o c", o=1)
                        dve.tensor_tensor(v, v, bcast(r[:, st:st + 1, :], [P, 1, b - a]), ALU.mult
                                          ).then_inc(z_normed, 1)
            dve.wait_ge(rope_ready, 2)
            with dve.Fori(0, T // 2) as i:
                z_norms(i, False)

            kr = Z[:, :, C_KR:Z_COLS]
            link(dve, dve.tensor_tensor(kr, kr, bcast(g_kr[:, :].rearrange("p (o c) -> p o c", o=1), [P, T, ROPE]),
                                        ALU.mult))
            r1, r2 = kr[:, :, 0:RH], kr[:, :, RH:ROPE]
            link(dve, dve.tensor_tensor(kr_rot[:, :, 0:RH], r1, cos_t[:, :, :], ALU.mult))
            link(dve, dve.tensor_tensor(kr_rot[:, :, RH:ROPE], r2, cos_t[:, :, :], ALU.mult))
            link(dve, dve.tensor_tensor(r1, r1, sin_t[:, :, :], ALU.mult))
            link(dve, dve.tensor_tensor(r2, r2, sin_t[:, :, :], ALU.mult))
            link(dve, dve.tensor_tensor(kr_rot[:, :, 0:RH], kr_rot[:, :, 0:RH], r2, ALU.subtract))
            link(dve, dve.tensor_tensor(kr_rot[:, :, RH:ROPE], kr_rot[:, :, RH:ROPE], r1, ALU.add))

            dve.wait_ge(pos_landed, 16)
            dve.wait_ge(ka_pad_ready, 2)
            dve.tensor_copy(pos_row[:, CHUNK:], pos_row_i[:, :]).then_inc(pos_ready, 1)
            dve.wait_ge(dist_abs, T)
            link(dve, dve.memset(dist[0:CHUNK, :, 2 * CHUNK:WIN], MASKED))
            link(dve, dve.memset(dist[CHUNK:P, :, 0:CHUNK], MASKED))
            link(dve, dve.memset(dist[0:CHUNK, 0, 0:CHUNK], MASKED))

            def a_scores(u):
                t, v, s = u // 2, u % 2, u % 2
                dve.wait_ge(a_qk_done, u + 1)
                if u >= 2:
                    dve.wait_ge(a_ptf_done, u - 1)
                if u >= 4:
                    dve.wait_ge(a_pth_done, u - 3)
                for g in range(A_GROUP):
                    dve.scalar_tensor_tensor(out=scA[:, s, g, 0:WIN], in0=dist[:, t, :],
                                             scalar=-SLOPES[A_GROUP * v + g],
                                             in1=PS[:, 2 * s + g % 2, 256 * (g // 2):256 * (g // 2) + WIN],
                                             op0=ALU.mult, op1=ALU.add)
                steps[0] += 1
                dve.tensor_copy(scA[:, s, :, WIN:WIN + 1],
                                sink_r[:, A_GROUP * v:A_GROUP * (v + 1)].rearrange("p (g o) -> p g o", o=1)
                                ).then_inc(dve_step, 1)
                dve.wait_ge(dve_step, steps[0])
                dve.tensor_reduce(a_nmax[:, s, :], scA[:, s, :, 0:WIN + 1], AX.X, ALU.max, negate=True
                                  ).then_inc(a_sc_ready, 1)

            def a_half(u):
                s = u % 2
                dve.wait_ge(a_exp_done, A_GROUP * (u + 1))
                link(dve, dve.reciprocal(a_rsum[:, s, :], a_sum[:, s, :]))
                if u >= 2:
                    dve.wait_ge(a_pth_done, u - 1)
                    dve.wait_ge(a_pv_done, u - 1)
                    dve.tensor_copy(ptA_half[s][0:CHUNK, :, :].rearrange("p g q -> p (g q)"), PS[0:CHUNK, 5, :]
                                    ).then_inc(a_pth_ready, 1)

            def a_y(u):
                t, v, s = u // 2, u % 2, u % 2
                dve.wait_ge(a_pv_done, u + 1)
                o = yA[:, t, v * 256:(v + 1) * 256].rearrange("p (g c) -> p g c", c=A_DIM)
                dve.tensor_tensor(o, PS[:, 6 + s, 0:256].rearrange("p (g c) -> p g c", c=A_DIM),
                                  bcast(a_rsum[:, s, :].rearrange("p (g o) -> p g o", o=1), [P, A_GROUP, A_DIM]),
                                  ALU.mult).then_inc(a_y_ready, 1)
            for u in range(2 * T + 2):
                if u < 2 * T:
                    a_scores(u)
                if 1 <= u <= 2 * T:
                    a_half(u - 1)
                if u >= 2:
                    a_y(u - 2)

            w0 = 0
            for g in range(B_GROUPS):
                for n in range(T):
                    hh, i = n // 4, n % 4
                    m = g * T + n
                    kv = PS[:, 2 * i + 1, :].rearrange("p (h c) -> p h c", c=P)
                    dve.wait_ge(b_nat_ready, 2 * m + 2)
                    dve.wait_ge(b_squared, 2 * m + 2)
                    dve.tensor_copy(vB[:, n, :, :], kv[:, :, NOPE:P]).then_inc(b_v_ready, 1)
                    if n % 4 == 0 and m:
                        dve.wait_ge(b_ms_ready, 2 * (m // 4))
                    dve.tensor_reduce(b_ss[:, i, 0:B_GROUP], sqB[:, 0:B_GROUP * QK].rearrange("p (h c) -> p h c", c=QK),
                                      AX.X, ALU.add).then_inc(b_summed, 1)
                    dve.tensor_reduce(b_ss[:, i, B_GROUP:], sqB[:, B_GROUP * QK:].rearrange("p (h c) -> p h c", c=NOPE),
                                      AX.X, ALU.add).then_inc(b_summed, 1)
                    if i < 3:
                        continue
                    ts = slice(4 * hh, 4 * hh + 4)
                    q, k = q_nat[hh], k_nat[hh]
                    dve.wait_ge(b_summed, 2 * (m + 1))
                    link(dve, dve.tensor_tensor(b_ss[:, :, B_GROUP:], b_ss[:, :, B_GROUP:],
                                                bcast(z_ss[:, ts, ST_KR:ST_KR + 1], [P, 4, B_GROUP]), ALU.add))
                    if m >= 4:
                        dve.wait_ge(b_rstd_ready, m // 4)
                    dve.tensor_scalar(b_ms[:, :, :], b_ss[:, :, :], 1.0 / QK, EPS, ALU.mult, ALU.add
                                      ).then_inc(b_ms_ready, 2)
                    dve.wait_ge(b_rstd_ready, m // 4 + 1)
                    for v in range(4):
                        rq = b_rstd[:, v, 0:B_GROUP].rearrange("p (h o) -> p h o", o=1)
                        rk = b_rstd[:, v, B_GROUP:].rearrange("p (h o) -> p h o", o=1)
                        dve.tensor_tensor(q[:, v, :, :], q[:, v, :, :], bcast(rq, [P, B_GROUP, QK]), ALU.mult)
                        dve.tensor_tensor(k[:, v, :, 0:NOPE], k[:, v, :, 0:NOPE], bcast(rk, [P, B_GROUP, NOPE]), ALU.mult)
                        kr_b = kr_rot[:, 4 * hh + v, :].rearrange("p (o c) -> p o c", o=1)
                        link(dve, dve.tensor_tensor(k[:, v, :, NOPE:QK], bcast(kr_b, [P, B_GROUP, ROPE]),
                                                    bcast(rk, [P, B_GROUP, ROPE]), ALU.mult))
                        gr = bcast(g_qr[:, :].rearrange("p (o c) -> p o c", o=1), [P, B_GROUP, ROPE])
                        link(dve, dve.tensor_tensor(q[:, v, :, NOPE:QK], q[:, v, :, NOPE:QK], gr, ALU.mult))
                        c3 = bcast(cos_t[:, 4 * hh + v, :].rearrange("p (o c) -> p o c", o=1), [P, B_GROUP, RH])
                        s3 = bcast(sin_t[:, 4 * hh + v, :].rearrange("p (o c) -> p o c", o=1), [P, B_GROUP, RH])
                        q1, q2 = q[:, v, :, NOPE:NOPE + RH], q[:, v, :, NOPE + RH:QK]
                        a0, a1, a2, a3 = [r[:, v, :, :] for r in rtmp]
                        dve.tensor_tensor(a0, q1, c3, ALU.mult)
                        dve.tensor_tensor(a1, q2, s3, ALU.mult)
                        dve.tensor_tensor(a2, q1, s3, ALU.mult)
                        link(dve, dve.tensor_tensor(a3, q2, c3, ALU.mult))
                        dve.tensor_tensor(q1, a0, a1, ALU.subtract)
                        last = dve.tensor_tensor(q2, a2, a3, ALU.add)
                        if v < 3:
                            link(dve, last)
                    last.then_inc(b_normed, 1)
                for n in range(16):
                    m = 16 * g + n
                    hh, what, h = n // 8, (n % 8) // 4, n % 4
                    if what == 1:
                        dve.wait_ge(bT_done, m + 1)
                        dve.tensor_copy(kbT[0:QK, h, hh * HALF:(hh + 1) * HALF], PS[0:QK, n % 8, :]
                                        ).then_inc(kbT_ready, 1)

                def b_max(w):
                    s, i = w % 2, w % T
                    dve.wait_ge(b_qk_done, w + 1)
                    sc = pair(2 * s)
                    link(dve, dve.memset(sc[0:CHUNK, i * P + CHUNK:(i + 1) * P], -MASKED))
                    if w >= 2:
                        dve.wait_ge(b_exp_done, w - 1)
                    dve.tensor_reduce(b_nmax[:, s:s + 1], sc[:, 0:(i + 1) * P], AX.X, ALU.max, negate=True
                                      ).then_inc(b_max_ready, 1)

                def b_pt1(w):
                    s, i = w % 2, w % T
                    dve.wait_ge(b_exp_done, w + 1)
                    link(dve, dve.reciprocal(b_rsum[:, s:s + 1], b_sum[:, s:s + 1]))
                    if i >= 4:
                        dve.wait_ge(b_pt1_done, 4 * (w // T) + i - 3)
                        if w >= 2:
                            dve.wait_ge(b_pv_done, w - 1)
                        dve.tensor_copy(ptB[s][:, 4:i + 1, :].rearrange("p k q -> p (k q)"),
                                        PS[:, 5, 0:(i - 3) * P]).then_inc(b_pt1_ready, 1)

                def b_y(w):
                    s, h, i = w % 2, w // T, w % T
                    dve.wait_ge(b_pv_done, w + 1)
                    dve.tensor_scalar(yB[:, i, h * V_DIM:(h + 1) * V_DIM], PS[:, 6 + s, 0:V_DIM],
                                      b_rsum[:, s:s + 1], None, ALU.mult).then_inc(b_y_ready, 1)
                n_w = B_GROUP * T
                for k in range(n_w + 2):
                    if k < n_w:
                        b_max(w0 + k)
                    if 1 <= k <= n_w:
                        b_pt1(w0 + k - 1)
                    if k >= 2:
                        b_y(w0 + k - 2)
                w0 += n_w

            for n in range(16):
                h, j = n // 8, n % 8
                cols = slice(h * HALF, (h + 1) * HALF)
                dve.wait_ge(yT_hi_done, n + 1)
                dve.tensor_tensor(yT_lo[:, j, cols], PS[:, n % 8, :], yT_hi[:, j, cols], ALU.subtract
                                  ).then_inc(yT_ready, 1)

            def merge(i, first):
                for s in range(2):
                    d = 2 * i + s
                    dve.wait_ge(branch_done, 2 * d + 2)
                    dve.tensor_tensor(gated_a[:, :], pair(4 * s), gate[:, d, :], ALU.mult).then_inc(gated_step, 1)
                    dve.tensor_tensor(gated_b[:, :], pair(4 * s + 2), gate[:, d + KD, :], ALU.mult
                                      ).then_inc(gated_step, 1)
                    dve.wait_ge(gated_step, 2 * d + 2)
                    if not (first and s == 0):
                        dve.wait_ge(mT_hi_done, d)
                    dve.tensor_tensor(merged[:, :], gated_a[:, :], gated_b[:, :], ALU.add).then_inc(merged_ready, 1)
                    dve.wait_ge(mT_hi_done, d + 1)
                    dve.tensor_tensor(mT_lo[:, d, :], merged[:, :], mT_hi[:, d, :], ALU.subtract
                                      ).then_inc(mT_ready, 1)
            peeled(dve, KD // 2, merge)

            for n in range(2 * T):
                r, t = n // T, n % T
                dve.wait_ge(o_done, n + 1)
                if r == 0:
                    dve.wait_ge(xr_landed[t], 16)
                else:
                    dve.wait_ge(xr_added, T)
                dve.tensor_tensor(xr[:, t, :], pair(2 * (n % 4)), xr[:, t, :], ALU.add).then_inc(xr_added, 1)
                if r == 1 and t % 4 == 3:
                    h = t // 4
                    ts = slice(4 * h, 4 * h + 4)
                    dve.wait_ge(x2_squared, 4 * (h + 1))
                    dve.tensor_scalar(x_ms[:, ts], x_ss[:, ts], 1.0 / D, EPS, ALU.mult, ALU.add
                                      ).then_inc(x2_ms_ready, 1)
            for t in range(T):
                if t % 4 == 0:
                    dve.wait_ge(x2_rstd_ready, t // 4 + 1)
                dve.tensor_scalar(x_norm[:, t, :], xr[:, t, :], x_rstd[:, t:t + 1], None, ALU.mult
                                  ).then_inc(x2_normed, 1)
            for n in range(2 * KD):
                h, j = n // KD, n % KD
                cols = slice(h * HALF, (h + 1) * HALF)
                dve.wait_ge(h2T_hi_done, n + 1)
                dve.scalar_tensor_tensor(out=h2T_lo[:, j, cols], in0=PS[:, n % 8, :], scalar=g_mlp_c[:, j:j + 1],
                                         in1=h2T_hi[:, j, cols], op0=ALU.mult, op1=ALU.subtract
                                         ).then_inc(h2T_ready, 1)

            def ff_vec(g, first):
                for j in range(GROUP):
                    for h in range(2):
                        cols = slice(h * HALF, (h + 1) * HALF)
                        n = 8 * g + 2 * j + h
                        dve.wait_ge(relu_ready, n + 1)
                        if not (first and j == 0):
                            dve.wait_ge(uT_ready, n - 1)
                        dve.tensor_tensor(relu_sq[:, cols], relu_t[:, cols], relu_t[:, cols], ALU.mult
                                          ).then_inc(relu_sq_ready, 1)
                    for h in range(2):
                        cols = slice(h * HALF, (h + 1) * HALF)
                        n = 8 * g + 2 * j + h
                        dve.wait_ge(uT_hi_done, n + 1)
                        dve.tensor_tensor(uT_lo[:, j, cols], relu_sq[:, cols], uT_hi[:, j, cols], ALU.subtract
                                          ).then_inc(uT_ready, 1)
                for t in range(T):
                    dve.wait_ge(down_done, T * g + t + 1)
                    if t == 0 and not first:
                        dve.wait_ge(x3_added, T * g)
                    dve.tensor_tensor(xr[:, t, :], pair(4 + 2 * (t % 2)), xr[:, t, :], ALU.add
                                      ).then_inc(x3_added, 1)
            peeled(dve, FF_GROUPS, ff_vec)


_INS = ['x', 'positions', 'g_mix', 'w_in', 'b_gate', 'g_qa', 'g_ka', 'sinks_a', 'g_cq', 'g_ckv', 'w_uq', 'w_ukv',
        'g_qb', 'g_kb', 'w_branch_a', 'w_branch_b', 'w_out', 'g_mlp', 'w_ff1', 'w_ff2']


def kernel(**inputs):
    import concourse.bacc as bacc
    from concourse.bass_utils import run_bass_kernel_spmd

    nc = bacc.Bacc("TRN2", target_bir_lowering=False, num_devices=1)
    arrays, args = {}, []
    for name in _INS:
        a = np.ascontiguousarray(inputs[name])
        arrays["in_" + name] = a
        args.append(nc.dram_tensor("in_" + name, a.shape, mybir.dt.from_np(a.dtype), kind="ExternalInput").ap())
    args.append(nc.dram_tensor("out_0", (1, S, D), F32, kind="ExternalOutput").ap())
    build(nc, *args)
    r = run_bass_kernel_spmd(nc, [arrays], core_ids=[0])
    return r.results[0]["out_0"]
```

```python
from contextlib import ExitStack

import numpy as np
import concourse.bass as bass
from concourse import mybir

F32 = mybir.dt.float32
F32R = mybir.dt.float32r
I32 = mybir.dt.int32
ACT = mybir.ActivationFunctionType
ALU = mybir.AluOpType
AX = mybir.AxisListType

P = 128
S = 1024
D = 1024
T = S // P
KD = D // P
HALF = S // 2
EPS = 1e-6

A_HEADS, A_KV, A_DIM = 8, 2, 64
A_GROUP = A_HEADS // A_KV
CHUNK = 64
WIN = 3 * CHUNK
B_HEADS, NOPE, ROPE, V_DIM = 8, 64, 32, 64
QK = NOPE + ROPE
RH = ROPE // 2
B_GROUP = 2
B_GROUPS = B_HEADS // B_GROUP
Q_RANK, KV_RANK = 256, 128
D_FF = 4 * D

C_Q, C_K, C_END = 0, 512, 640
R_V, R_CQ, R_CKV, R_KR, R_END = 0, 128, 384, 512, 544
Z_COLS = C_END + R_END
CHUNKS = ((0, 320), (320, 320), (640, 272), (912, 272))
ZC = max(w for _, w in CHUNKS)
Z_CHUNKS = len(CHUNKS)
Z_RAW = 3
SUM_SLOTS = 4
N_STAT = A_HEADS + A_KV + 3
ST_CQ, ST_CKV, ST_KR = 10, 11, 12

GROUP = 4
FF_GROUPS = D_FF // P // GROUP
MASKED = 1e30
N_A = 2 * T
N_B = B_HEADS * T
N_UNITS = N_A + N_B
BG_UNITS = B_GROUP * T
SLOPES = [float(2.0 ** (-8.0 * (h + 1) / A_HEADS)) for h in range(A_HEADS)]
INV_FREQ = (np.float32(10000.0) ** (-np.arange(RH, dtype=np.float32) / np.float32(RH))).tolist()
TWO_PI = 2.0 * np.pi
PI_A = float(np.float32(6.28125))
PI_B = float(np.float32(np.round((TWO_PI - PI_A) * 2 ** 20) / 2 ** 20))
PI_C = float(np.float32(TWO_PI - PI_A - PI_B))
ROUND = float(1.5 * 2 ** 23)
SIN_MAX = 3.1415925


def build(nc, x, positions, g_mix, w_in, b_gate, g_qa, g_ka, sinks_a, g_cq, g_ckv,
          w_uq, w_ukv, g_qb, g_kb, w_branch_a, w_branch_b, w_out, g_mlp, w_ff1, w_ff2, out):
    x_d = x[0].rearrange("(t p) d -> t p d", p=P)
    out_d = out[0].rearrange("(t p) d -> t p d", p=P)
    w_in_d, w_uq_d, w_ukv_d = w_in[0], w_uq[0], w_ukv[0]
    w_out_d, w1_d, w2_d = w_out[0], w_ff1[0], w_ff2[0]

    with ExitStack() as ctx:
        def sem(name):
            return ctx.enter_context(nc.semaphore(name))

        def const(name, shape, dt=F32):
            return ctx.enter_context(nc.sbuf_tensor(name, shape, dt))

        ident = const("ident", [P, P])
        g_mix_c = const("g_mix_c", [P, KD])
        g_mlp_c = const("g_mlp_c", [P, KD])
        b_gate_c = const("b_gate_c", [P, 2 * KD])
        g_qa_c = const("g_qa_c", [P, 1])
        g_ka_c = const("g_ka_c", [P, 1])
        gqk_a = const("gqk_a", [P, 1])
        g_cq_c = const("g_cq_c", [P, 2])
        g_ckv_c = const("g_ckv_c", [P, 1])
        g_qb_c = const("g_qb_c", [P, 1])
        g_kb_c = const("g_kb_c", [P, 1])
        gqk_b = const("gqk_b", [P, 1])
        g_qr = const("g_qr", [P, ROPE])
        g_kr = const("g_kr", [P, ROPE])
        sink_r = const("sink_r", [P, A_HEADS])
        pos_i = const("pos_i", [P, T], I32)
        pos_c = const("pos_c", [P, T])
        inv_f = const("inv_f", [P, RH])
        minus_half = const("minus_half", [P, T * N_STAT])
        x_ss = const("x_ss", [P, T])
        x_ms = const("x_ms", [P, T])
        x_rstd = const("x_rstd", [P, T])
        z_ss = const("z_ss", [P, T, N_STAT])
        z_ms = const("z_ms", [P, T, N_STAT])
        z_rstd = const("z_rstd", [P, T, N_STAT])
        b_ss = const("b_ss", [P, T, 2 * B_GROUP])
        b_ms = const("b_ms", [P, T, 2 * B_GROUP])
        b_rstd = const("b_rstd", [P, T, 2 * B_GROUP])
        cos_t = const("cos_t", [P, T, RH])
        sin_t = const("sin_t", [P, T, RH])
        kr_rot = const("kr_rot", [P, T, ROPE])
        a_nmax = const("a_nmax", [P, 2, A_GROUP])
        a_sum = const("a_sum", [P, SUM_SLOTS, A_GROUP])
        a_rsum = const("a_rsum", [P, SUM_SLOTS, A_GROUP])
        b_nmax = const("b_nmax", [P, 2])
        b_sum = const("b_sum", [P, SUM_SLOTS])
        b_rsum = const("b_rsum", [P, SUM_SLOTS])

        BASE = 8
        probe = ctx.enter_context(nc.sbuf_tensor("base_gap", [P, 8], F32))
        used = 0
        for t_ in (ident, g_mix_c, g_mlp_c, b_gate_c, g_qa_c, g_ka_c, gqk_a, g_cq_c, g_ckv_c, g_qb_c, g_kb_c,
                   gqk_b, g_qr, g_kr, sink_r, pos_i, pos_c, inv_f, minus_half, x_ss, x_ms, x_rstd, z_ss, z_ms,
                   z_rstd, b_ss, b_ms, b_rstd, cos_t, sin_t, kr_rot, a_nmax, a_sum, a_rsum, b_nmax, b_sum,
                   b_rsum, probe):
            n = 4
            for v in t_.shape[1:]:
                n *= v
            used += (n + 31) // 32 * 32
        assert used <= BASE * 1024, used

        def place(name, kib, shape, dt=F32):
            pad = int(kib * 1024) - used
            with nc.sbuf_tensor("pad_" + name, [P, pad // 4], F32):
                with nc.sbuf_tensor(name, shape, dt) as t_:
                    return t_

        hT_hi = place("hT_hi", 8, [P, KD, S], F32R)
        hT_lo = place("hT_lo", 40, [P, KD, S], F32R)
        x_in = place("x_in", 72, [P, T, D])
        zw_hi = [place(f"zw_hi{i}", 104 + 20 * i, [P, KD, ZC], F32R) for i in range(2)]
        zw_lo = [place(f"zw_lo{i}", 114 + 20 * i, [P, KD, ZC], F32R) for i in range(2)]
        z_raw = [place(f"z_raw{i}", 144 + 5 * i, [P, 4, ZC]) for i in range(Z_RAW)]
        sq = place("sq", 160, [P, Z_COLS])
        Zq = place("Zq", 168, [P, T, C_END])
        Zr = place("Zr", 188, [P, T, R_END])
        gw_hi = [place(f"gw_hi{i}", 72 + 8 * i, [P, KD, P], F32R) for i in range(2)]
        gw_lo = [place(f"gw_lo{i}", 76 + 8 * i, [P, KD, P], F32R) for i in range(2)]
        gate = place("gate", 88, [P, 2 * KD, S])
        g_raw = [place(f"g_raw{i}", 152 + 4 * i, [P, KD, P]) for i in range(2)]
        k_dup = place("k_dup", 160, [P, T, A_KV, 2, A_DIM])
        rope_tmp = [place(f"rope_tmp{i}", 165 + 0.5 * i, [P, T, RH]) for i in range(6)]
        qaT = place("qaT", 8, [P, 4, S])
        kaT = place("kaT", 24, [P, A_KV, CHUNK + S])
        dist = place("dist", 32.5, [P, T, WIN])
        scA = place("scA", 38.5, [P, 2, A_GROUP, WIN + 2])
        ptA_full = [place(f"ptA_full{i}", 44.75 + 4 * i, [P, A_GROUP, P]) for i in range(2)]
        ptA_half = [place(f"ptA_half{i}", 46.75 + 4 * i, [P, A_GROUP, P]) for i in range(2)]
        v_odd = place("v_odd", 52.75, [P, T, A_KV * A_DIM])
        cqT = place("cqT", 56.75, [P, 2, S])
        ckvT = place("ckvT", 64.75, [P, S])
        pos_row_i = place("pos_row_i", 79, [P, S], I32)
        pos_row = place("pos_row", 83, [P, CHUNK + S])
        yA = place("yA", 152, [P, T, A_HEADS * A_DIM])
        w_at = [68.75, 200]
        wuq = [place(f"wuq{i}", w_at[i], [P, 2, B_GROUP * QK]) for i in range(2)]
        wukv = [place(f"wukv{i}", w_at[i] + 1.5, [P, B_GROUP * (NOPE + V_DIM)]) for i in range(2)]
        sqB = place("sqB", 71.25, [P, B_GROUP * (QK + NOPE + V_DIM)])
        rtmp = [place(f"rtmp{i}", 73 + 0.5 * i, [P, 4, B_GROUP, RH]) for i in range(4)]
        vB = [place(f"vB{i}", (75, 188, 202.5)[i], [P, T, B_GROUP, V_DIM]) for i in range(3)]
        qbT = [place(f"qbT{i}", (79, 24)[i], [P, B_GROUP, S]) for i in range(2)]
        kbT = [place(f"kbT{i}", (180, 32)[i], [P, B_GROUP, S]) for i in range(2)]
        q_nat = place("q_nat", 168, [P, T, B_GROUP, QK])
        k_nat = place("k_nat", 174, [P, T, B_GROUP, QK])
        yB = place("yB", 8, [P, T, B_HEADS * V_DIM])
        prB = [place(f"prB{i}", 40 + 4 * i, [P, S]) for i in range(2)]
        ptB = [place(f"ptB{i}", 48 + 4 * i, [P, T, P]) for i in range(2)]
        yT_hi = place("yT_hi", 24, [P, 8, S], F32R)
        yT_lo = place("yT_lo", 56, [P, 8, S], F32R)
        raw = [place(f"raw{i}", 192 + 4 * i, [P, 1024]) for i in range(2)]
        bw_at = [168, 176]
        bw_hi = [place(f"bw_hi{i}", bw_at[i], [P, 8, P], F32R) for i in range(2)]
        bw_lo = [place(f"bw_lo{i}", bw_at[i] + 4, [P, 8, P], F32R) for i in range(2)]
        gated_a = place("gated_a", 184, [P, S])
        gated_b = place("gated_b", 188, [P, S])
        merged = place("merged", 200, [P, S])
        mT_hi = place("mT_hi", 88, [P, KD, S], F32R)
        mT_lo = place("mT_lo", 120, [P, KD, S], F32R)
        ow_at = [8, 16, 152, 160, 24, 32, 40, 48]
        ow_hi = [place(f"ow_hi{i}", ow_at[i], [P, D], F32R) for i in range(8)]
        ow_lo = [place(f"ow_lo{i}", ow_at[i] + 4, [P, D], F32R) for i in range(8)]
        xr = place("xr", 56, [P, T, D])
        x_norm = place("x_norm", 152, [P, T, D])
        sq2 = place("sq2", 200, [P, D])
        h2T_hi = place("h2T_hi", 88, [P, KD, S], F32R)
        h2T_lo = place("h2T_lo", 120, [P, KD, S], F32R)
        uT_hi = place("uT_hi", 8, [P, GROUP, S], F32R)
        uT_lo = place("uT_lo", 24, [P, GROUP, S], F32R)
        relu_t = place("relu_t", 40, [P, S])
        relu_sq = place("relu_sq", 44, [P, S])
        w1_at = [184, 48]
        w1_hi = [place(f"w1_hi{i}", w1_at[i], [P, KD, P], F32R) for i in range(2)]
        w1_lo = [place(f"w1_lo{i}", w1_at[i] + 4, [P, KD, P], F32R) for i in range(2)]
        w2_hi = [place(f"w2_hi{i}", 152 + 8 * i, [P, D], F32R) for i in range(4)]
        w2_lo = [place(f"w2_lo{i}", 156 + 8 * i, [P, D], F32R) for i in range(4)]

        PS = ctx.enter_context(nc.psum_tensor("PS", [P, 8, 512], F32))
        PSF = PS[:, :, :].rearrange("p b n -> p (b n)")

        def pair(b):
            return PSF[:, 512 * b:512 * b + 1024]

        g_mix_in = sem("g_mix_in")
        const_in = sem("const_in")
        ident_ready = sem("ident_ready")
        const_ready = sem("const_ready")
        x_landed = [sem(f"x_landed{t}") for t in range(T)]
        x_squared = sem("x_squared")
        x_ms_ready = sem("x_ms_ready")
        x_rstd_ready = sem("x_rstd_ready")
        x_normed = sem("x_normed")
        xT_done = sem("xT_done")
        hT_hi_done = sem("hT_hi_done")
        hT_ready = sem("hT_ready")
        zraw_landed = [sem(f"zraw_landed{i}") for i in range(Z_RAW)]
        zw_hi_done = sem("zw_hi_done")
        zw_ready = sem("zw_ready")
        z_tile_done = sem("z_tile_done")
        z_evac = sem("z_evac")
        graw_landed = [sem(f"graw_landed{i}") for i in range(2)]
        gw_hi_done = sem("gw_hi_done")
        gw_ready = sem("gw_ready")
        gate_done = sem("gate_done")
        gate_ready = sem("gate_ready")
        z_squared = sem("z_squared")
        z_summed = sem("z_summed")
        z_ms_ready = sem("z_ms_ready")
        z_rstd_ready = sem("z_rstd_ready")
        z_normed = sem("z_normed")
        angle_ready = sem("angle_ready")
        rope_ready = sem("rope_ready")
        aT_done = sem("aT_done")
        aT_act_ready = sem("aT_act_ready")
        aT_dve_ready = sem("aT_dve_ready")
        ka_pad_ready = sem("ka_pad_ready")
        pos_landed = sem("pos_landed")
        pos_ready = sem("pos_ready")
        dist_dve_done = sem("dist_dve_done")
        dist_act_done = sem("dist_act_done")
        dist_ready = sem("dist_ready")
        v_odd_ready = sem("v_odd_ready")
        qk_done = sem("qk_done")
        max_ready = sem("max_ready")
        exp_done = sem("exp_done")
        pt0_done = sem("pt0_done")
        pt1_done = sem("pt1_done")
        pt0_ready = sem("pt0_ready")
        pt1_ready = sem("pt1_ready")
        pv_done = sem("pv_done")
        y_ready = sem("y_ready")
        wb_landed = [sem(f"wb_landed{i}") for i in range(2)]
        proj_done = sem("proj_done")
        proj_act_read = sem("proj_act_read")
        proj_dve_read = sem("proj_dve_read")
        b_summed = sem("b_summed")
        b_ms_ready = sem("b_ms_ready")
        b_rstd_ready = sem("b_rstd_ready")
        b_rotary = sem("b_rotary")
        b_normed = sem("b_normed")
        bT_done = sem("bT_done")
        qbT_ready = sem("qbT_ready")
        kbT_ready = sem("kbT_ready")
        yT_done = sem("yT_done")
        yT_hi_done = sem("yT_hi_done")
        yT_ready = sem("yT_ready")
        raw_landed = [sem(f"raw_landed{i}") for i in range(2)]
        bw_hi_done = sem("bw_hi_done")
        bw_ready = sem("bw_ready")
        branch_done = sem("branch_done")
        merged_ready = sem("merged_ready")
        mT_hi_done = sem("mT_hi_done")
        mT_ready = sem("mT_ready")
        ow_hi_done = sem("ow_hi_done")
        ow_ready = sem("ow_ready")
        xr_landed = [sem(f"xr_landed{t}") for t in range(T)]
        o_done = sem("o_done")
        xr_added = sem("xr_added")
        x2_squared = sem("x2_squared")
        x2_ms_ready = sem("x2_ms_ready")
        x2_rstd_ready = sem("x2_rstd_ready")
        x2_normed = sem("x2_normed")
        x2T_done = sem("x2T_done")
        h2T_hi_done = sem("h2T_hi_done")
        h2T_ready = sem("h2T_ready")
        w1_hi_done = sem("w1_hi_done")
        w1_ready = sem("w1_ready")
        w2_hi_done = sem("w2_hi_done")
        w2_ready = sem("w2_ready")
        up_done = sem("up_done")
        relu_ready = sem("relu_ready")
        relu_sq_ready = sem("relu_sq_ready")
        uT_hi_done = sem("uT_hi_done")
        uT_ready = sem("uT_ready")
        down_done = sem("down_done")
        x3_added = sem("x3_added")
        out_written = sem("out_written")
        dve_step = sem("dve_step")
        gated_step = sem("gated_step")

        steps = [0]

        def link(dve, instruction):
            steps[0] += 1
            instruction.then_inc(dve_step, 1)
            dve.wait_ge(dve_step, steps[0])

        Y_BANKS = (0, 1, 2, 3, 4, 5, 7, 6)

        A_BY_ACT = (0, 1, 2, 3, 6, 7, 8, 9, 12, 13, 14)
        A_BY_DVE = (4, 5, 10, 11, 15, 16, 17)

        def small_transposed(n):
            h = n // 6 if n < 12 else (n - 12) // 3
            j = n % 6 if n < 12 else n % 3
            cols = slice(h * HALF, (h + 1) * HALF)
            if n < 12 and j < 4:
                return qaT[:, j, cols], gqk_a[:, 0:1]
            if n < 12:
                return kaT[:, j - 4, CHUNK + h * HALF:CHUNK + (h + 1) * HALF], None
            if j < 2:
                return cqT[:, j, cols], g_cq_c[:, j:j + 1]
            return ckvT[:, cols], g_ckv_c[:, 0:1]

        def wait_small_read(eng, n):
            if n in A_BY_ACT:
                eng.wait_ge(aT_act_ready, A_BY_ACT.index(n) + 1)
            else:
                eng.wait_ge(aT_dve_ready, A_BY_DVE.index(n) + 1)

        def x_bank(h, j):
            return j if h == 0 else 4 + j % 4

        def bcast(ap, shape):
            return ap.to_broadcast(shape)

        def peeled(eng, n, body):
            body(0, True)
            with eng.Fori(1, n) as i:
                body(i, False)

        def unrolled(n, body):
            for i in range(n):
                body(i, i == 0)

        def kind(k):
            return ("A", k // 2, k % 2) if k < N_A else ("B", (k - N_A) // T, T - 1 - (k - N_A) % T)

        def has_pt1(k):
            b, m, n = kind(k)
            return m > 0 if b == "A" else n >= 4

        def pt1_count(k):
            return sum(has_pt1(j) for j in range(k + 1))

        def wait_scores_read(eng, k):
            if kind(k)[0] == "A":
                eng.wait_ge(max_ready, k + 1)
            else:
                eng.wait_ge(exp_done, k + 1)

        def preparation(k):
            g = k // BG_UNITS
            return (g, k % BG_UNITS) if g < B_HEADS // B_GROUP else None

        n_const = [0]

        block = ctx.enter_context(nc.Block())

        @block.sync
        def _(sp):
            def z_load(n):
                (c0, w), kh = CHUNKS[n // 2], n % 2
                if n >= Z_RAW:
                    sp.wait_ge(zw_ready, n - Z_RAW + 1)
                sp.dma_start(z_raw[n % Z_RAW][:, :, 0:w],
                             w_in_d[kh * 512:(kh + 1) * 512, c0:c0 + w].rearrange("(k p) n -> p k n", p=P)
                             ).then_inc(zraw_landed[n % Z_RAW], 16)

            for t in range(T):
                sp.dma_start(x_in[:, t, :], x_d[t]).then_inc(x_landed[t], 16)
                if t == 3:
                    z_load(0)
                    z_load(1)
            for n in range(2, 2 * Z_CHUNKS):
                z_load(n)
            sp.wait_ge(zw_ready, 2 * Z_CHUNKS)

            def gate_loads(i, first):
                for s in range(2):
                    if not first:
                        sp.wait_ge(gw_ready, 2 * i + s - 1)
                    sp.dma_start(g_raw[s][:, :, :],
                                 w_in_d[:, bass.ds(Z_COLS + (2 * i + s) * P, P)].rearrange("(k p) n -> p k n", p=P)
                                 ).then_inc(graw_landed[s], 16)
            peeled(sp, KD, gate_loads)

            sp.wait_ge(gate_done, 2 * KD)
            sp.dma_start(pos_row_i[:, :], positions[0:1, :].partition_broadcast(P)).then_inc(pos_landed, 16)

            def group_load(g):
                s = g % 2
                sp.dma_start(wuq[s][:, :, :], w_uq_d[:, g * B_GROUP * QK:(g + 1) * B_GROUP * QK].rearrange(
                    "(k p) n -> p k n", p=P)).then_inc(wb_landed[s], 16)
                sp.dma_start(wukv[s][:, :], w_ukv_d[:, g * B_GROUP * P:(g + 1) * B_GROUP * P]).then_inc(wb_landed[s], 16)
            group_load(0)
            sp.wait_ge(pv_done, N_A)
            group_load(1)
            for g in (2, 3):
                sp.wait_ge(proj_done, T * (g - 1))
                group_load(g)


            def branch_loads(i, first):
                for s in range(2):
                    if not first:
                        sp.wait_ge(bw_ready, 2 * i + s - 1)
                    dst = raw[s][:, :].rearrange("p (k n) -> p k n", n=P)
                    cols = bass.ds((2 * i + s) * P, P)
                    sp.dma_start(dst[:, 0:4, :], w_branch_a[0][:, cols].rearrange("(k p) n -> p k n", p=P)
                                 ).then_inc(raw_landed[s], 16)
                    sp.dma_start(dst[:, 4:8, :], w_branch_b[0][:, cols].rearrange("(k p) n -> p k n", p=P)
                                 ).then_inc(raw_landed[s], 16)
            peeled(sp, KD // 2, branch_loads)

            def out_load(k):
                if k < 2:
                    sp.wait_ge(bw_ready, KD - 1 + k)
                else:
                    sp.wait_ge(ow_ready, k - 1)
                sp.dma_start(raw[k % 2][:, :], w_out_d[k * P:(k + 1) * P, :]).then_inc(raw_landed[k % 2], 16)

            for k in range(4):
                out_load(k)
            sp.wait_ge(branch_done, 2 * KD)
            for t in range(T):
                sp.dma_start(xr[:, t, :], x_d[t]).then_inc(xr_landed[t], 16)
            for k in range(4, 8):
                out_load(k)

            def ff_loads(g, first):
                def load(n, what, j, *split):
                    for s_, v in split:
                        sp.wait_ge(s_, v)
                    if what == 1:
                        src = w1_d[:, bass.ds(g * (GROUP * P) + j * P, P)].rearrange("(k p) n -> p k n", p=P)
                        dst = raw[n % 2][:, :].rearrange("p (k n) -> p k n", n=P)
                    else:
                        src = w2_d[bass.ds(g * (GROUP * P) + j * P, P), :]
                        dst = raw[n % 2][:, :]
                    sp.dma_start(dst, src).then_inc(raw_landed[n % 2], 16)
                load(0, 1, 0, (ow_ready, 7) if first else (w1_ready, 4 * g))
                load(1, 1, 1, (ow_ready, 8) if first else (w2_ready, 4 * g))
                load(2, 2, 0, (w1_ready, 4 * g + 1))
                load(3, 2, 1, (w1_ready, 4 * g + 2))
                load(4, 1, 2, (w2_ready, 4 * g + 1))
                load(5, 2, 2, (w2_ready, 4 * g + 2))
                load(6, 1, 3, (w1_ready, 4 * g + 3))
                load(7, 2, 3, (w2_ready, 4 * g + 3))
            peeled(sp, FF_GROUPS, ff_loads)
            for t in range(T):
                sp.wait_ge(x3_added, T * (FF_GROUPS - 1) + t + 1)
                sp.dma_start(out_d[t], xr[:, t, :]).then_inc(out_written, 16)
            sp.wait_ge(out_written, 16 * T)

        @block.gpsimd
        def _(pool):
            pool.memset(ident[:, :], 0.0).then_inc(ident_ready, 1)
            pool.memset(minus_half[:, :], -0.5).then_inc(const_ready, 1)
            for i in range(RH):
                pool.memset(inv_f[:, i:i + 1], INV_FREQ[i]).then_inc(const_ready, 1)
            pool.wait_ge(ident_ready, 1)
            pool.affine_select(out=ident[:, :], in_=ident[:, :], compare_op=ALU.not_equal, fill=1.0, base=0,
                               pattern=[[-1, P]], channel_multiplier=1).then_inc(ident_ready, 1)

            def split(raw_ap, hi_ap, lo_ap, hi_done, count, ready):
                pool.tensor_scalar(hi_ap, raw_ap, 1.0, 1.0, ALU.mult, ALU.mult).then_inc(hi_done, 1)
                pool.wait_ge(hi_done, count)
                pool.tensor_tensor(lo_ap, raw_ap, hi_ap, ALU.subtract).then_inc(ready, 1)

            def power(out_ap, in_ap, n, shape):
                e = minus_half[:, 0:n]
                if len(shape) == 3:
                    e = e.rearrange("p (a b) -> p a b", b=shape[2])
                return pool.tensor_tensor(out_ap, in_ap, e, ALU.pow)

            def z_split(n):
                c, kh = n // 2, n % 2
                w = CHUNKS[c][1]
                pool.wait_ge(zraw_landed[n % Z_RAW], 16 * (n // Z_RAW + 1))
                if c >= 2:
                    pool.wait_ge(z_tile_done, T * (c - 1))
                split(z_raw[n % Z_RAW][:, :, 0:w], zw_hi[c % 2][:, 4 * kh:4 * kh + 4, 0:w],
                      zw_lo[c % 2][:, 4 * kh:4 * kh + 4, 0:w], zw_hi_done, n + 1, zw_ready)

            pool.wait_ge(const_ready, 1 + RH)
            for h in range(2):
                pool.wait_ge(x_ms_ready, h + 1)
                power(x_rstd[:, 4 * h:4 * h + 4], x_ms[:, 4 * h:4 * h + 4], 4, (P, 4)).then_inc(x_rstd_ready, 1)
                if h == 0:
                    z_split(0)
                    z_split(1)
            for n in range(2, 2 * Z_CHUNKS):
                z_split(n)

            pool.wait_ge(hT_ready, 2 * KD)

            def gate_split(u):
                s = u % 2
                pool.wait_ge(graw_landed[s], 16 * (u // 2 + 1))
                if u >= 2:
                    pool.wait_ge(gate_done, u - 1)
                split(g_raw[s][:, :, :], gw_hi[s][:, :, :], gw_lo[s][:, :, :], gw_hi_done, u + 1, gw_ready)
            for u in range(2 * KD):
                gate_split(u)
                if u % 2 and 2 < u < 2 * 5 + 1:
                    i = u // 2 - 1
                    pool.wait_ge(z_ms_ready, 4 * (i + 1))
                    power(z_rstd[:, 2 * i:2 * i + 2, :], z_ms[:, 2 * i:2 * i + 2, :], 2 * N_STAT, (P, 2, N_STAT)
                          ).then_inc(z_rstd_ready, 1)

            pool.wait_ge(gate_done, 2 * KD)
            pool.memset(kaT[:, :, 0:CHUNK], 0.0).then_inc(ka_pad_ready, 1)
            pool.memset(pos_row[:, 0:CHUNK], 0.0).then_inc(ka_pad_ready, 1)
            pool.wait_ge(dist_dve_done, 1)
            pool.wait_ge(dist_act_done, 1)
            pool.memset(dist[0:CHUNK, :, 2 * CHUNK:WIN], MASKED).then_inc(dist_ready, 1)
            pool.memset(dist[CHUNK:P, :, 0:CHUNK], MASKED).then_inc(dist_ready, 1)
            pool.memset(dist[0:CHUNK, 0, 0:CHUNK], MASKED).then_inc(dist_ready, 1)

            for n in range(2 * B_HEADS // B_GROUP):
                ts = slice(4 * (n % 2), 4 * (n % 2) + 4)
                pool.wait_ge(b_ms_ready, n + 1)
                pool.wait_ge(proj_act_read, 4 * (n + 1))
                power(b_rstd[:, ts, :], b_ms[:, ts, :], 4 * 2 * B_GROUP, (P, 4, 2 * B_GROUP)).then_inc(b_rstd_ready, 1)
                pool.wait_ge(b_rstd_ready, n + 1)
                r = b_rstd[:, ts, :].rearrange("p t (h o) -> p t h o", o=1)
                rq, rk = r[:, :, 0:B_GROUP, :], r[:, :, B_GROUP:, :]
                pool.tensor_tensor(q_nat[:, ts, :, :], q_nat[:, ts, :, :], bcast(rq, [P, 4, B_GROUP, QK]), ALU.mult
                                   ).then_inc(b_rotary, 1)
                pool.tensor_tensor(k_nat[:, ts, :, 0:NOPE], k_nat[:, ts, :, 0:NOPE],
                                   bcast(rk, [P, 4, B_GROUP, NOPE]), ALU.mult)
                kr_b = kr_rot[:, ts, :].rearrange("p t (o c) -> p t o c", o=1)
                pool.tensor_tensor(k_nat[:, ts, :, NOPE:QK], bcast(kr_b, [P, 4, B_GROUP, ROPE]),
                                   bcast(rk, [P, 4, B_GROUP, ROPE]), ALU.mult)
                q = q_nat[:, ts, :, NOPE:QK]
                gr = g_qr[:, :].rearrange("p (a o c) -> p a o c", a=1, o=1)
                pool.wait_ge(b_rotary, 3 * n + 1)
                pool.tensor_tensor(q, q, bcast(gr, [P, 4, B_GROUP, ROPE]), ALU.mult).then_inc(b_rotary, 1)
                c4 = bcast(cos_t[:, ts, :].rearrange("p t (o c) -> p t o c", o=1), [P, 4, B_GROUP, RH])
                s4 = bcast(sin_t[:, ts, :].rearrange("p t (o c) -> p t o c", o=1), [P, 4, B_GROUP, RH])
                q1, q2 = q[:, :, :, 0:RH], q[:, :, :, RH:ROPE]
                a0, a1, a2, a3 = [v[:, :, :, :] for v in rtmp]
                pool.wait_ge(b_rotary, 3 * n + 2)
                pool.tensor_tensor(a0, q1, c4, ALU.mult)
                pool.tensor_tensor(a1, q2, s4, ALU.mult)
                pool.tensor_tensor(a2, q1, s4, ALU.mult)
                pool.tensor_tensor(a3, q2, c4, ALU.mult).then_inc(b_rotary, 1)
                pool.wait_ge(b_rotary, 3 * n + 3)
                pool.tensor_tensor(q1, a0, a1, ALU.subtract)
                pool.tensor_tensor(q2, a2, a3, ALU.add).then_inc(b_normed, 1)

            def branch_splits(i, first):
                for s in range(2):
                    d = 2 * i + s
                    pool.wait_ge(raw_landed[s], 32 * (i + 1))
                    if first:
                        pool.wait_ge(pv_done, N_UNITS - BG_UNITS)
                        pool.wait_ge(bT_done, 8 * B_HEADS // B_GROUP)
                    if not first:
                        pool.wait_ge(branch_done, 2 * (d - 1))
                    split(raw[s][:, :].rearrange("p (k n) -> p k n", n=P), bw_hi[s][:, :, :], bw_lo[s][:, :, :],
                          bw_hi_done, d + 1, bw_ready)
            unrolled(KD // 2, branch_splits)

            for k in range(8):
                pool.wait_ge(raw_landed[k % 2], 32 * 4 + 16 * (k // 2 + 1))
                if k == 0:
                    pool.wait_ge(yT_done, 16)
                if k == 4:
                    pool.wait_ge(branch_done, 2 * KD)
                split(raw[k % 2][:, :], ow_hi[k][:, :], ow_lo[k][:, :], ow_hi_done, k + 1, ow_ready)

            def ff_splits(g, first):
                landed = 32 * 4 + 16 * 4 + 64 * g

                def unit(n, what, j):
                    pool.wait_ge(raw_landed[n % 2], landed + 16 * (n // 2 + 1))
                    if what == 1:
                        if first and j < 2:
                            if j == 0:
                                pool.wait_ge(merged_ready, KD)
                            else:
                                pool.wait_ge(o_done, 2 * T)
                        else:
                            pool.wait_ge(up_done, 4 * g + j - 1)
                        split(raw[n % 2][:, :].rearrange("p (k n) -> p k n", n=P), w1_hi[j % 2][:, :, :],
                              w1_lo[j % 2][:, :, :], w1_hi_done, 4 * g + j + 1, w1_ready)
                    else:
                        if j == 0:
                            if first:
                                pool.wait_ge(x2T_done, 2 * KD)
                            else:
                                pool.wait_ge(down_done, T * g)
                        split(raw[n % 2][:, :], w2_hi[j][:, :], w2_lo[j][:, :], w2_hi_done, 4 * g + j + 1, w2_ready)
                unit(0, 1, 0)
                if first:
                    for h in range(2):
                        pool.wait_ge(x2_ms_ready, h + 1)
                        power(x_rstd[:, 4 * h:4 * h + 4], x_ms[:, 4 * h:4 * h + 4], 4, (P, 4)
                              ).then_inc(x2_rstd_ready, 1)
                unit(1, 1, 1)
                unit(2, 2, 0)
                unit(3, 2, 1)
                unit(4, 1, 2)
                unit(5, 2, 2)
                unit(6, 1, 3)
                unit(7, 2, 3)
            unrolled(FF_GROUPS, ff_splits)

        @block.scalar
        def _(act):
            def load(dst, src):
                act.dma_start(dst, src).then_inc(const_in, 16)
                n_const[0] += 1

            def column(v, a, b):
                return v[0, a:b].rearrange("(p o) -> p o", o=1)

            with nc.allow_non_contiguous_dma(reason="gains and biases, a few KiB in all"):
                act.dma_start(g_mix_c[:, :], g_mix[0].rearrange("(j p) -> p j", p=P)).then_inc(g_mix_in, 16)

            def x_squares(h):
                for t in range(4 * h, 4 * h + 4):
                    act.wait_ge(x_landed[t], 16)
                    if t >= 1:
                        act.wait_ge(x_squared, t)
                    act.activation(sq[:, 0:D], x_in[:, t, :], ACT.Square, accum_out=x_ss[:, t:t + 1]
                                   ).then_inc(x_squared, 1)

            def hT_high(h):
                for j in range(KD):
                    act.wait_ge(xT_done, KD * h + j + 1)
                    act.activation(hT_hi[:, j, h * HALF:(h + 1) * HALF], PS[:, x_bank(h, j), :], ACT.Copy,
                                   scale=g_mix_c[:, j:j + 1]).then_inc(hT_hi_done, 1)

            def z_out(c, t):
                act.wait_ge(z_tile_done, T * c + t + 1)
                c0, w = CHUNKS[c]
                dst = Zq[:, t, c0:c0 + w] if c0 < C_END else Zr[:, t, c0 - C_END:c0 - C_END + w]
                act.activation(dst, PS[:, t, 0:w], ACT.Copy).then_inc(z_evac, 1)

            x_squares(0)
            act.wait_ge(g_mix_in, 16)
            hT_high(0)
            x_squares(1)
            with nc.allow_non_contiguous_dma(reason="gains and biases, a few KiB in all"):
                load(pos_i[:, :], positions[0].rearrange("(t p) -> p t", p=P))
                load(b_gate_c[:, :], b_gate[0].rearrange("(j p) -> p j", p=P))
                load(g_mlp_c[:, :], g_mlp[0].rearrange("(j p) -> p j", p=P))
                load(g_cq_c[:, :], g_cq[0].rearrange("(j p) -> p j", p=P))
                load(g_ckv_c[:, :], column(g_ckv, 0, KV_RANK))
                for r in (0, A_DIM):
                    load(g_qa_c[r:r + A_DIM, :], column(g_qa, 0, A_DIM))
                    load(g_ka_c[r:r + A_DIM, :], column(g_ka, 0, A_DIM))
                load(g_qb_c[0:NOPE, :], column(g_qb, 0, NOPE))
                load(g_kb_c[0:NOPE, :], column(g_kb, 0, NOPE))
                load(g_qr[:, :], g_qb[0:1, NOPE:QK].partition_broadcast(P))
                load(g_kr[:, :], g_kb[0:1, NOPE:QK].partition_broadcast(P))
                load(sink_r[:, :], sinks_a[0:1, :].partition_broadcast(P))
            for t in range(4):
                z_out(0, t)
            hT_high(1)
            for t in range(4, T):
                z_out(0, t)
            for c in range(1, Z_CHUNKS):
                for t in range(T):
                    z_out(c, t)

            act.wait_ge(angle_ready, 2)
            act.activation(sin_t[:, :, :], rope_tmp[4][:, :, :], ACT.Sin).then_inc(rope_ready, 1)
            act.activation(cos_t[:, :, :], rope_tmp[5][:, :, :], ACT.Sin).then_inc(rope_ready, 1)
            act.wait_ge(const_in, 16 * n_const[0])

            act.wait_ge(z_evac, Z_CHUNKS * T)

            def gate_a(i, first):
                for s in range(2):
                    u = 2 * i + s
                    act.wait_ge(gate_done, u + 1)
                    act.activation(gate[:, u, :], pair(2 * s), ACT.Sigmoid, bias=b_gate_c[:, bass.ds(u, 1)]
                                   ).then_inc(gate_ready, 1)
                    if not (first and s == 0):
                        act.wait_ge(z_summed, 4 * u)
                    act.activation(sq[:, 0:C_END], Zq[:, u, :], ACT.Square).then_inc(z_squared, 1)
                    act.activation(sq[:, C_END:], Zr[:, u, :], ACT.Square).then_inc(z_squared, 1)

            def gate_b(i, first):
                for s in range(2):
                    u = 2 * i + s + KD
                    act.wait_ge(gate_done, u + 1)
                    act.activation(gate[:, u, :], pair(2 * s), ACT.Sigmoid, bias=b_gate_c[:, bass.ds(u, 1)]
                                   ).then_inc(gate_ready, 1)
            peeled(act, KD // 2, gate_a)
            with act.Fori(0, KD // 2) as i:
                gate_b(i, False)

            act.wait_ge(ka_pad_ready, 2)
            for n in A_BY_ACT:
                if n == 6:
                    act.wait_ge(pos_ready, 1)
                    for t in range(T // 2, T):
                        ins = act.activation(dist[:, t, :], pos_row[:, t * P:t * P + WIN], ACT.Abs, scale=-1.0,
                                             bias=pos_c[:, t:t + 1])
                    ins.then_inc(dist_act_done, 1)
                act.wait_ge(aT_done, n + 1)
                dst, gain = small_transposed(n)
                act.activation(dst, PS[:, (n + 4) % 8, :], ACT.Copy, scale=gain).then_inc(aT_act_ready, 1)
            act.activation(v_odd[0:CHUNK, :, :], Zr[CHUNK:P, :, R_V:R_CQ], ACT.Copy
                           ).then_inc(v_odd_ready, 1)

            def q_of_a_group(k):
                if preparation(k) is None:
                    return
                g, p = preparation(k)
                m = T * g + p
                if p < T:
                    act.wait_ge(proj_done, m + 1)
                    if k == 0:
                        act.wait_ge(aT_done, 12)
                    if p == 0 and g:
                        act.wait_ge(bT_done, 8 * g)
                    act.activation(q_nat[:, p, :, :].rearrange("p h c -> p (h c)"), PS[:, 7, 0:B_GROUP * QK], ACT.Copy)
                    if m:
                        act.wait_ge(b_summed, 2 * m)
                    act.activation(sqB[:, :], PS[:, 7, 0:B_GROUP * (QK + P)], ACT.Square).then_inc(proj_act_read, 1)
                elif (p // 2) % 2 == 0:
                    hh, h = (p - 8) // 4, p % 2
                    act.wait_ge(bT_done, 8 * g + p - 7)
                    if g == 1 and p == 8:
                        act.wait_ge(pv_done, N_A)
                    if g >= 2 and p == 8:
                        act.wait_ge(qk_done, N_A + BG_UNITS * (g - 1))
                    act.activation(qbT[g % 2][0:QK, h, hh * HALF:(hh + 1) * HALF], PS[0:QK, 7, :], ACT.Copy,
                                   scale=gqk_b[0:QK, 0:1]).then_inc(qbT_ready, 1)

            def exps(k):
                b, m, n = kind(k)
                s = k % 2
                act.wait_ge(max_ready, k + 1)
                ss = k % SUM_SLOTS
                if k >= SUM_SLOTS:
                    act.wait_ge(y_ready, k - SUM_SLOTS + 1)
                if b == "A":
                    for g in range(A_GROUP):
                        ins = act.activation(scA[:, s, g, 0:WIN + 1], scA[:, s, g, 0:WIN + 1], ACT.Exp,
                                             bias=a_nmax[:, s, g:g + 1], accum_out=a_sum[:, ss, g:g + 1])
                    ins.then_inc(exp_done, 1)
                else:
                    if k == N_A:
                        act.wait_ge(pv_done, N_A)
                    act.activation(prB[s][:, 0:(n + 1) * P], pair(2 * s)[:, 0:(n + 1) * P], ACT.Exp,
                                   bias=b_nmax[:, s:s + 1], accum_out=b_sum[:, ss:ss + 1]).then_inc(exp_done, 1)

            def pt_first(k):
                b, m, n = kind(k)
                act.wait_ge(pt0_done, k + 1)
                if k >= 2:
                    act.wait_ge(pv_done, k - 1)
                if b == "A":
                    act.activation(ptA_full[k % 2][:, :, :].rearrange("p g q -> p (g q)"), PS[:, 4, :], ACT.Copy
                                   ).then_inc(pt0_ready, 1)
                else:
                    w = min(n + 1, 4)
                    act.activation(ptB[k % 2][:, 0:w, :].rearrange("p k q -> p (k q)"), PS[:, 4, 0:w * P], ACT.Copy
                                   ).then_inc(pt0_ready, 1)
            for k in range(N_UNITS + 1):
                if k == N_A:
                    pt_first(k - 1)
                if k < N_UNITS:
                    q_of_a_group(k)
                if k >= 1 and k != N_A:
                    pt_first(k - 1)
                if k < N_UNITS:
                    exps(k)

            act.wait_ge(pv_done, N_UNITS)
            for n in range(16):
                j, h = n // 2, n % 2
                act.wait_ge(yT_done, n + 1)
                act.activation(yT_hi[:, j, h * HALF:(h + 1) * HALF], PS[:, Y_BANKS[n % 8], :], ACT.Copy
                               ).then_inc(yT_hi_done, 1)

            with act.Fori(0, KD) as d:
                act.wait_ge(merged_ready, d + 1)
                act.activation(mT_hi[:, d, :], merged[:, :], ACT.Copy).then_inc(mT_hi_done, 1)

            for t in range(T):
                act.wait_ge(xr_added, T + t + 1)
                if t:
                    act.wait_ge(x2_squared, t)
                act.activation(sq2[:, :], xr[:, t, :], ACT.Square, accum_out=x_ss[:, t:t + 1]).then_inc(x2_squared, 1)
            for n in range(2 * KD):
                h, j = n // KD, n % KD
                act.wait_ge(x2T_done, n + 1)
                if n == 0:
                    act.wait_ge(o_done, 2 * T)
                act.activation(h2T_hi[:, j, h * HALF:(h + 1) * HALF], PS[:, n % 8, :], ACT.Copy,
                               scale=g_mlp_c[:, j:j + 1]).then_inc(h2T_hi_done, 1)

            def ff_up(g, first):
                for j in range(GROUP):
                    act.wait_ge(up_done, 4 * g + j + 1)
                    for h in range(2):
                        cols = slice(h * HALF, (h + 1) * HALF)
                        if not (first and j == 0):
                            act.wait_ge(relu_sq_ready, 8 * g + 2 * j - 1 + h)
                        act.activation(relu_t[:, cols], PS[:, 2 * (j % 2) + h, :], ACT.Relu).then_inc(relu_ready, 1)
                    for h in range(2):
                        cols = slice(h * HALF, (h + 1) * HALF)
                        act.wait_ge(relu_sq_ready, 8 * g + 2 * j + h + 1)
                        if j == 0 and h == 0:
                            if first:
                                act.wait_ge(x2T_done, 2 * KD)
                                act.wait_ge(o_done, 2 * T)
                            else:
                                act.wait_ge(down_done, T * g)
                        act.activation(uT_hi[:, j, cols], relu_sq[:, cols], ACT.Copy).then_inc(uT_hi_done, 1)
            peeled(act, FF_GROUPS, ff_up)

        @block.tensor
        def _(pe):
            def split_products(w_hi, w_lo, x_hi, x_lo, outs, k, first, last):
                passes = ((w_hi, x_hi), (w_hi, x_lo), (w_lo, x_hi))
                ins = None
                for n, (st, mv) in enumerate(passes):
                    for o, cut in outs:
                        ins = pe.matmul(o, st, cut(mv), start=first and n == 0, stop=last and n == 2)
                return ins

            def transpose_tiles(bank, tiles, rows=P):
                ins = None
                for i, ap in enumerate(tiles):
                    ins = pe.transpose(PS[0:rows, bank, i * P:(i + 1) * P], ap, ident[:, :])
                return ins

            def x_transposes(h):
                pe.wait_ge(x_normed, 4 * (h + 1))
                for j in range(KD):
                    if h:
                        pe.wait_ge(hT_ready, KD if j < 4 else KD + j - 3)
                    transpose_tiles(x_bank(h, j), [x_in[:, 4 * h + i, j * P:(j + 1) * P] for i in range(4)]
                                    ).then_inc(xT_done, 1)

            def z_tile(c, t):
                w = CHUNKS[c][1]
                if c:
                    pe.wait_ge(z_evac, T * (c - 1) + t + 1)
                rows = slice(t * P, (t + 1) * P)
                for k in range(KD):
                    if t == 0 and k % 4 == 0:
                        pe.wait_ge(zw_ready, 2 * c + k // 4 + 1)
                    ins = split_products(hT_hi[:, k, rows], hT_lo[:, k, rows], zw_hi[c % 2][:, k, 0:w],
                                         zw_lo[c % 2][:, k, 0:w], [(PS[:, t, 0:w], lambda m: m)],
                                         k, k == 0, k == KD - 1)
                ins.then_inc(z_tile_done, 1)

            pe.wait_ge(ident_ready, 2)
            x_transposes(0)
            pe.wait_ge(hT_ready, KD)
            for t in range(4):
                z_tile(0, t)
            x_transposes(1)
            pe.wait_ge(hT_ready, 2 * KD)
            for t in range(4, T):
                z_tile(0, t)
            for c in range(1, Z_CHUNKS):
                for t in range(T):
                    z_tile(c, t)

            halves = [lambda m: m[:, 0:HALF], lambda m: m[:, HALF:S]]

            pe.wait_ge(z_evac, Z_CHUNKS * T)

            def gates(i, first):
                for s in range(2):
                    u = 2 * i + s
                    pe.wait_ge(gw_ready, u + 1)
                    if not first:
                        pe.wait_ge(gate_ready, u - 1)
                    for k in range(KD):
                        ins = split_products(gw_hi[s][:, k, :], gw_lo[s][:, k, :], hT_hi[:, k, :], hT_lo[:, k, :],
                                             [(PS[:, 2 * s + h, :], halves[h]) for h in range(2)],
                                             k, k == 0, k == KD - 1)
                    ins.then_inc(gate_done, 1)
            peeled(pe, KD, gates)

            pe.wait_ge(z_normed, 5 * T)
            n = 0

            def small_transpose(tiles):
                nonlocal n
                if n == 4:
                    pe.wait_ge(gate_ready, 2 * KD)
                if n >= 8:
                    wait_small_read(pe, n - 8)
                transpose_tiles((n + 4) % 8, tiles).then_inc(aT_done, 1)
                n += 1
            for h in range(2):
                ts = range(4 * h, 4 * h + 4)
                for p in range(4):
                    small_transpose([Zq[:, t, p * P:(p + 1) * P] for t in ts])
                for v in range(A_KV):
                    small_transpose([k_dup[:, t, v, :, :].rearrange("p a b -> p (a b)") for t in ts])
            for h in range(2):
                ts = range(4 * h, 4 * h + 4)
                for j in range(2):
                    small_transpose([Zr[:, t, R_CQ + j * P:R_CQ + (j + 1) * P] for t in ts])
                small_transpose([Zr[:, t, R_CKV:R_KR] for t in ts])
            for m in (A_BY_ACT[-1], A_BY_DVE[-1]):
                wait_small_read(pe, m)

            def group_step(k):
                if preparation(k) is None:
                    return
                g, p = preparation(k)
                m = T * g + p
                if p < T:
                    rows = slice(p * P, (p + 1) * P)
                    if p == 0:
                        pe.wait_ge(wb_landed[g % 2], 32 * (g // 2 + 1))
                        if g:
                            pe.wait_ge(qbT_ready, 4 * g)
                            pe.wait_ge(kbT_ready, 4 * g)
                    else:
                        pe.wait_ge(proj_act_read, m)
                        pe.wait_ge(proj_dve_read, m)
                    for c in range(2):
                        pe.matmul(PS[:, 7, 0:B_GROUP * QK], cqT[:, c, rows], wuq[g % 2][:, c, :],
                                  start=c == 0, stop=c == 1)
                    pe.matmul(PS[:, 7, B_GROUP * QK:B_GROUP * (QK + P)], ckvT[:, rows], wukv[g % 2][:, :],
                              start=True, stop=True).then_inc(proj_done, 1)
                else:
                    hh, what, h = (p - 8) // 4, (p // 2) % 2, p % 2
                    if p == 8:
                        pe.wait_ge(proj_act_read, T * (g + 1))
                        pe.wait_ge(proj_dve_read, T * (g + 1))
                    elif (p - 1) // 2 % 2 == 0:
                        pe.wait_ge(qbT_ready, 4 * g + 2 * ((p - 9) // 4) + (p - 1) % 2 + 1)
                    else:
                        pe.wait_ge(kbT_ready, 4 * g + 2 * ((p - 9) // 4) + (p - 1) % 2 + 1)
                    if p % 4 == 0:
                        pe.wait_ge(b_normed, 2 * g + hh + 1)
                    src = (q_nat, k_nat)[what]
                    transpose_tiles(7, [src[:, 4 * hh + i, h, :] for i in range(4)], QK).then_inc(bT_done, 1)

            def scores(k):
                b, m, n = kind(k)
                s = k % 2
                if k >= 2:
                    wait_scores_read(pe, k - 2)
                if b == "A":
                    for g in range(A_GROUP):
                        head = A_GROUP * n + g
                        r = A_DIM * (head % 2)
                        ins = pe.matmul(PS[:, 2 * s + g % 2, 256 * (g // 2):256 * (g // 2) + WIN],
                                        qaT[r:r + A_DIM, head // 2, m * P:(m + 1) * P],
                                        kaT[r:r + A_DIM, n, m * P:m * P + WIN], start=True, stop=True)
                else:
                    gs, h = (m // B_GROUP) % 2, m % B_GROUP
                    if (k - N_A) % BG_UNITS == 0:
                        pe.wait_ge(qbT_ready, 4 * (m // B_GROUP + 1))
                        pe.wait_ge(kbT_ready, 4 * (m // B_GROUP + 1))
                    for c in range(0, (n + 1) * P, 512):
                        w = min(512, (n + 1) * P - c)
                        ins = pe.matmul(pair(2 * s)[:, c:c + w], qbT[gs][0:QK, h, n * P:(n + 1) * P],
                                        kbT[gs][0:QK, h, c:c + w], start=True, stop=True)
                ins.then_inc(qk_done, 1)

            def p_transposes(k):
                b, m, n = kind(k)
                s = k % 2
                pe.wait_ge(exp_done, k + 1)
                if k >= 1:
                    pe.wait_ge(pt0_ready, k)
                if b == "A":
                    for g in range(A_GROUP):
                        ins = pe.transpose(PS[:, 4, g * P:(g + 1) * P], scA[:, s, g, CHUNK:WIN], ident[:, :])
                else:
                    for c in range(min(n + 1, 4)):
                        ins = pe.transpose(PS[:, 4, c * P:(c + 1) * P], prB[s][:, c * P:(c + 1) * P], ident[:, :])
                ins.then_inc(pt0_done, 1)
                if not has_pt1(k):
                    return
                if pt1_count(k - 1):
                    pe.wait_ge(pt1_ready, pt1_count(k - 1))
                if b == "A":
                    for g in range(A_GROUP):
                        ins = pe.transpose(PS[0:CHUNK, 5, g * P:(g + 1) * P], scA[:, s, g, 0:CHUNK], ident[:, :])
                else:
                    for c in range(4, n + 1):
                        ins = pe.transpose(PS[:, 5, (c - 4) * P:(c - 3) * P], prB[s][:, c * P:(c + 1) * P],
                                           ident[:, :])
                ins.then_inc(pt1_done, 1)

            def values(k):
                b, m, n = kind(k)
                s = k % 2
                pe.wait_ge(pt0_ready, k + 1)
                if has_pt1(k):
                    pe.wait_ge(pt1_ready, pt1_count(k))
                if k >= 1:
                    pe.wait_ge(y_ready, k)
                if k == 0:
                    pe.wait_ge(v_odd_ready, 1)
                if b == "A":
                    v = slice(n * A_DIM, (n + 1) * A_DIM)
                    for g in range(A_GROUP):
                        o = PS[:, 6, g * A_DIM:(g + 1) * A_DIM]
                        if m:
                            pe.matmul(o, ptA_half[s][0:CHUNK, g, :], v_odd[0:CHUNK, m - 1, v], start=True, stop=False)
                        ins = pe.matmul(o, ptA_full[s][:, g, :], Zr[:, m, v], start=m == 0, stop=True)
                else:
                    for c in range(n + 1):
                        ins = pe.matmul(PS[:, 6, 0:V_DIM], ptB[s][:, c, :], vB[(m // B_GROUP) % 3][:, c, m % B_GROUP, :],
                                        start=c == 0, stop=c == n)
                ins.then_inc(pv_done, 1)
            for k in range(N_UNITS + 2):
                if k == N_A:
                    scores(k)
                    values(k - 2)
                    p_transposes(k - 1)
                    values(k - 1)
                    group_step(k)
                    continue
                if k < N_UNITS:
                    scores(k)
                    group_step(k)
                if k >= 2 and k != N_A + 1:
                    values(k - 2)
                if 1 <= k <= N_UNITS:
                    p_transposes(k - 1)

            for n in range(16):
                j, h = n // 2, n % 2
                if n in (7, 8):
                    pe.wait_ge(y_ready, N_UNITS)
                if n >= 8:
                    pe.wait_ge(yT_ready, n - 7)
                src, jj = (yA, j) if j < 4 else (yB, j - 4)
                transpose_tiles(Y_BANKS[n % 8], [src[:, 4 * h + i, jj * P:(jj + 1) * P] for i in range(4)]
                                ).then_inc(yT_done, 1)

            def branches(i, first):
                for s in range(2):
                    d = 2 * i + s
                    pe.wait_ge(bw_ready, d + 1)
                    if not first:
                        pe.wait_ge(merged_ready, d - 1)
                    for b in range(2):
                        if first and s == 0:
                            pe.wait_ge(yT_ready, (10, 16)[b])
                        for k in range(4):
                            kk = 4 * b + k
                            ins = split_products(bw_hi[s][:, kk, :], bw_lo[s][:, kk, :], yT_hi[:, kk, :],
                                                 yT_lo[:, kk, :],
                                                 [(PS[:, 4 * s + 2 * b + h, :], halves[h]) for h in range(2)],
                                                 k, k == 0, k == 3)
                        ins.then_inc(branch_done, 1)
            peeled(pe, KD // 2, branches)

            for n in range(2 * T):
                r, t = n // T, n % T
                if t == 0:
                    pe.wait_ge(mT_ready, 4 * (r + 1))
                if n < 4:
                    pe.wait_ge(merged_ready, KD - 1 if n < 2 else KD)
                if n >= 4:
                    pe.wait_ge(xr_added, n - 3)
                rows = slice(t * P, (t + 1) * P)
                for k in range(4 * r, 4 * r + 4):
                    if t == 0:
                        pe.wait_ge(ow_ready, k + 1)
                    ins = split_products(mT_hi[:, k, rows], mT_lo[:, k, rows], ow_hi[k][:, :], ow_lo[k][:, :],
                                         [(PS[:, 2 * (n % 4) + h, :], halves[h]) for h in range(2)],
                                         k, k == 4 * r, k == 4 * r + 3)
                ins.then_inc(o_done, 1)

            for n in range(2 * KD):
                h, j = n // KD, n % KD
                if j == 0:
                    pe.wait_ge(x2_normed, 4 * (h + 1))
                if n < 8:
                    pe.wait_ge(xr_added, 2 * T - 3 + n // 2)
                if n >= 8:
                    pe.wait_ge(h2T_ready, n - 7)
                transpose_tiles(n % 8, [x_norm[:, 4 * h + i, j * P:(j + 1) * P] for i in range(4)]
                                ).then_inc(x2T_done, 1)

            def ff(g, first):
                for j in range(GROUP):
                    pe.wait_ge(w1_ready, 4 * g + j + 1)
                    if not (first and j < 2):
                        pe.wait_ge(relu_ready, 8 * g + 2 * j - 2)
                    elif j == 0:
                        pe.wait_ge(h2T_ready, KD + 2)
                    for hs in ((0,), (1,)) if first and j == 0 else ((0, 1),):
                        if first and j == 0:
                            pe.wait_ge(h2T_ready, KD * (hs[0] + 1))
                        for k in range(KD):
                            ins = split_products(w1_hi[j % 2][:, k, :], w1_lo[j % 2][:, k, :], h2T_hi[:, k, :],
                                                 h2T_lo[:, k, :],
                                                 [(PS[:, 2 * (j % 2) + h, :], halves[h]) for h in hs],
                                                 k, k == 0, k == KD - 1)
                    ins.then_inc(up_done, 1)
                for t in range(T):
                    rows = slice(t * P, (t + 1) * P)
                    if not (first and t < 2):
                        pe.wait_ge(x3_added, T * g + t - 1)
                    for j in range(GROUP):
                        if t == 0:
                            pe.wait_ge(w2_ready, 4 * g + j + 1)
                            pe.wait_ge(uT_ready, 8 * g + 2 * j + 1)
                        if t == 4 and j == 0:
                            pe.wait_ge(uT_ready, 8 * g + 8)
                        ins = split_products(uT_hi[:, j, rows], uT_lo[:, j, rows], w2_hi[j][:, :], w2_lo[j][:, :],
                                             [(PS[:, 4 + 2 * (t % 2) + h, :], halves[h]) for h in range(2)],
                                             j, j == 0, j == GROUP - 1)
                    ins.then_inc(down_done, 1)
            peeled(pe, FF_GROUPS, ff)

        @block.vector
        def _(dve):
            def x_norm_half(h):
                ts = slice(4 * h, 4 * h + 4)
                dve.wait_ge(x_squared, 4 * (h + 1))
                dve.tensor_scalar(x_ms[:, ts], x_ss[:, ts], 1.0 / D, EPS, ALU.mult, ALU.add).then_inc(x_ms_ready, 1)
                dve.wait_ge(x_rstd_ready, h + 1)
                for t in range(4 * h, 4 * h + 4):
                    dve.tensor_scalar(x_in[:, t, :], x_in[:, t, :], x_rstd[:, t:t + 1], None, ALU.mult
                                      ).then_inc(x_normed, 1)

            def hT_low(h):
                cols = slice(h * HALF, (h + 1) * HALF)
                for j in range(KD):
                    dve.wait_ge(hT_hi_done, KD * h + j + 1)
                    dve.scalar_tensor_tensor(out=hT_lo[:, j, cols], in0=PS[:, x_bank(h, j), :],
                                             scalar=g_mix_c[:, j:j + 1], in1=hT_hi[:, j, cols],
                                             op0=ALU.mult, op1=ALU.subtract).then_inc(hT_ready, 1)
            x_norm_half(0)
            dve.wait_ge(g_mix_in, 16)
            hT_low(0)
            x_norm_half(1)
            hT_low(1)

            dve.wait_ge(const_in, 16 * n_const[0])
            link(dve, dve.memset(gqk_b[:, :], QK ** -0.5))
            link(dve, dve.tensor_copy(pos_c[:, :], pos_i[:, :]))
            link(dve, dve.tensor_tensor(gqk_a[:, :], g_qa_c[:, :], g_ka_c[:, :], ALU.mult))
            link(dve, dve.tensor_scalar(gqk_a[:, :], gqk_a[:, :], A_DIM ** -0.5, None, ALU.mult))
            link(dve, dve.tensor_tensor(g_qb_c[0:NOPE, :], g_qb_c[0:NOPE, :], g_kb_c[0:NOPE, :], ALU.mult))
            link(dve, dve.tensor_tensor(gqk_b[0:NOPE, :], gqk_b[0:NOPE, :], g_qb_c[0:NOPE, :], ALU.mult))
            dve.wait_ge(const_ready, 1 + RH)
            ang, turns, part, _r, s_ang, c_ang = [r[:, :, :] for r in rope_tmp]
            full = [P, T, RH]
            link(dve, dve.tensor_tensor(ang, bcast(pos_c[:, :].rearrange("p (t o) -> p t o", o=1), full),
                                        bcast(inv_f[:, :].rearrange("p (o f) -> p o f", o=1), full), ALU.mult))
            for red, quarter in ((s_ang, 0.0), (c_ang, 0.25)):
                link(dve, dve.tensor_scalar(turns, ang, 1.0 / TWO_PI, quarter, ALU.mult, ALU.add))
                link(dve, dve.tensor_scalar(turns, turns, ROUND, ROUND, ALU.add, ALU.subtract))
                for pi_part in (PI_A, PI_B, PI_C):
                    link(dve, dve.tensor_scalar(part, turns, pi_part, None, ALU.mult))
                    link(dve, dve.tensor_tensor(red, ang if pi_part == PI_A else red, part, ALU.subtract))
                if quarter:
                    link(dve, dve.tensor_scalar(red, red, TWO_PI * quarter, None, ALU.add))
                dve.tensor_scalar(red, red, SIN_MAX, -SIN_MAX, ALU.min, ALU.max).then_inc(angle_ready, 1)

            def z_sums(i, first):
                for s in range(2):
                    t = 2 * i + s
                    dve.wait_ge(z_squared, 2 * (t + 1))
                    dve.tensor_reduce(z_ss[:, t, 0:ST_CQ], sq[:, 0:C_END].rearrange("p (h c) -> p h c", c=A_DIM), AX.X,
                                      ALU.add).then_inc(z_summed, 1)
                    for st, a, b in ((ST_CQ, R_CQ, R_CKV), (ST_CKV, R_CKV, R_KR), (ST_KR, R_KR, R_END)):
                        dve.tensor_reduce(z_ss[:, t, st:st + 1], sq[:, C_END + a:C_END + b], AX.X, ALU.add
                                          ).then_inc(z_summed, 1)
                dve.wait_ge(z_summed, 8 * i + 8)
                for a, b, width in ((0, ST_CQ, A_DIM), (ST_CQ, ST_CKV, Q_RANK), (ST_CKV, ST_KR, KV_RANK),
                                    (ST_KR, N_STAT, ROPE)):
                    dve.tensor_scalar(z_ms[:, bass.ds(2 * i, 2), a:b], z_ss[:, bass.ds(2 * i, 2), a:b], 1.0 / width,
                                      EPS, ALU.mult, ALU.add).then_inc(z_ms_ready, 1)
            with dve.Fori(0, T // 2) as i:
                z_sums(i, False)
            dve.wait_ge(z_rstd_ready, 4)

            def z_norms(i, first):
                for s in range(2):
                    t = 2 * i + s
                    q = Zq[:, t, 0:C_K].rearrange("p (h c) -> p h c", c=A_DIM)
                    k = Zq[:, t, C_K:C_END].rearrange("p (h c) -> p h c", c=A_DIM)
                    r = z_rstd[:, t, :].rearrange("p (n o) -> p n o", o=1)
                    dve.tensor_tensor(q, q, bcast(r[:, 0:A_HEADS, :], [P, A_HEADS, A_DIM]), ALU.mult
                                      ).then_inc(z_normed, 1)
                    for c in range(2):
                        dve.tensor_tensor(k_dup[:, t, :, c, :], k, bcast(r[:, A_HEADS:ST_CQ, :], [P, A_KV, A_DIM]),
                                          ALU.mult).then_inc(z_normed, 1)
                    for st, a, b in ((ST_CQ, R_CQ, R_CKV), (ST_CKV, R_CKV, R_KR)):
                        v = Zr[:, t, a:b].rearrange("p (o c) -> p o c", o=1)
                        dve.tensor_tensor(v, v, bcast(r[:, st:st + 1, :], [P, 1, b - a]), ALU.mult
                                          ).then_inc(z_normed, 1)
            dve.wait_ge(rope_ready, 2)
            with dve.Fori(0, T // 2) as i:
                z_norms(i, False)

            kr = Zr[:, :, R_KR:R_END]
            link(dve, dve.tensor_tensor(kr, kr, bcast(g_kr[:, :].rearrange("p (o c) -> p o c", o=1), [P, T, ROPE]),
                                        ALU.mult))
            r1, r2 = kr[:, :, 0:RH], kr[:, :, RH:ROPE]
            link(dve, dve.tensor_tensor(kr_rot[:, :, 0:RH], r1, cos_t[:, :, :], ALU.mult))
            link(dve, dve.tensor_tensor(kr_rot[:, :, RH:ROPE], r2, cos_t[:, :, :], ALU.mult))
            link(dve, dve.tensor_tensor(r1, r1, sin_t[:, :, :], ALU.mult))
            link(dve, dve.tensor_tensor(r2, r2, sin_t[:, :, :], ALU.mult))
            link(dve, dve.tensor_tensor(kr_rot[:, :, 0:RH], kr_rot[:, :, 0:RH], r2, ALU.subtract))
            link(dve, dve.tensor_tensor(kr_rot[:, :, RH:ROPE], kr_rot[:, :, RH:ROPE], r1, ALU.add))

            def small_read(n):
                dve.wait_ge(aT_done, n + 1)
                dst, gain = small_transposed(n)
                if gain is None:
                    dve.tensor_copy(dst, PS[:, (n + 4) % 8, :]).then_inc(aT_dve_ready, 1)
                else:
                    dve.tensor_scalar(dst, PS[:, (n + 4) % 8, :], gain, None, ALU.mult).then_inc(aT_dve_ready, 1)

            dve.wait_ge(pos_landed, 16)
            dve.wait_ge(ka_pad_ready, 2)
            dve.tensor_copy(pos_row[:, CHUNK:], pos_row_i[:, :]).then_inc(pos_ready, 1)
            dve.wait_ge(pos_ready, 1)
            for n in A_BY_DVE:
                if n == 10:
                    for t in range(T // 2):
                        ins = dve.tensor_scalar(dist[:, t, :], pos_row[:, t * P:t * P + WIN], pos_c[:, t:t + 1],
                                                None, ALU.subtract)
                    link(dve, ins)
                    d = dist[:, 0:T // 2, :]
                    dve.scalar_tensor_tensor(out=d, in0=d, scalar=-1.0, in1=d, op0=ALU.mult, op1=ALU.max
                                             ).then_inc(dist_dve_done, 1)
                small_read(n)
            dve.wait_ge(dist_ready, 3)

            def group_vec(k):
                if preparation(k) is None:
                    return
                g, p = preparation(k)
                m, sl = T * g + p, g % 2
                if p < T:
                    kv = PS[:, 7, B_GROUP * QK:B_GROUP * (QK + P)].rearrange("p (h c) -> p h c", c=P)
                    dve.wait_ge(proj_done, m + 1)
                    dve.wait_ge(proj_act_read, m + 1)
                    if p == 0 and g:
                        dve.wait_ge(bT_done, 8 * g)
                    if p == 0 and g == 1:
                        dve.wait_ge(pv_done, N_A)
                    if p == 0 and g >= 3:
                        dve.wait_ge(pv_done, N_A + BG_UNITS * (g - 2))
                    dve.tensor_copy(k_nat[:, p, :, 0:NOPE], kv[:, :, 0:NOPE])
                    dve.tensor_copy(vB[g % 3][:, p, :, :], kv[:, :, NOPE:P]).then_inc(proj_dve_read, 1)
                    if p == 0 and g:
                        dve.wait_ge(b_ms_ready, 2 * g)
                    nq = B_GROUP * QK
                    dve.tensor_reduce(b_ss[:, p, 0:B_GROUP], sqB[:, 0:nq].rearrange("p (h c) -> p h c", c=QK),
                                      AX.X, ALU.add).then_inc(b_summed, 1)
                    dve.tensor_reduce(b_ss[:, p, B_GROUP:],
                                      sqB[:, nq:].rearrange("p (h c) -> p h c", c=P)[:, :, 0:NOPE],
                                      AX.X, ALU.add).then_inc(b_summed, 1)
                elif (p // 2) % 2 == 1:
                    hh, h = (p - 8) // 4, p % 2
                    dve.wait_ge(bT_done, 8 * g + p - 7)
                    if g >= 2 and p == 10:
                        dve.wait_ge(qk_done, N_A + BG_UNITS * (g - 1))
                    dve.tensor_copy(kbT[sl][0:QK, h, hh * HALF:(hh + 1) * HALF], PS[0:QK, 7, :]
                                    ).then_inc(kbT_ready, 1)
                if p % 4 == 3 and p < T:
                    n, ts = 2 * g + p // 4, slice(p - 3, p + 1)
                    dve.wait_ge(b_summed, 2 * (m + 1))
                    link(dve, dve.tensor_tensor(b_ss[:, ts, B_GROUP:], b_ss[:, ts, B_GROUP:],
                                                bcast(z_ss[:, ts, ST_KR:ST_KR + 1], [P, 4, B_GROUP]), ALU.add))
                    if n >= 2:
                        dve.wait_ge(b_rstd_ready, n - 1)
                    dve.tensor_scalar(b_ms[:, ts, :], b_ss[:, ts, :], 1.0 / QK, EPS, ALU.mult, ALU.add
                                      ).then_inc(b_ms_ready, 1)

            def maxima(k):
                b, m, n = kind(k)
                s = k % 2
                dve.wait_ge(qk_done, k + 1)
                if b == "A":
                    if k >= 2:
                        dve.wait_ge(pt0_done, k - 1)
                        if has_pt1(k - 2):
                            dve.wait_ge(pt1_done, pt1_count(k - 2))
                    for g in range(A_GROUP):
                        dve.scalar_tensor_tensor(out=scA[:, s, g, 0:WIN], in0=dist[:, m, :],
                                                 scalar=-SLOPES[A_GROUP * n + g],
                                                 in1=PS[:, 2 * s + g % 2, 256 * (g // 2):256 * (g // 2) + WIN],
                                                 op0=ALU.mult, op1=ALU.add)
                    link(dve, dve.tensor_copy(scA[:, s, :, WIN:WIN + 1],
                                              sink_r[:, A_GROUP * n:A_GROUP * (n + 1)].rearrange(
                                                  "p (g o) -> p g o", o=1)))
                    dve.tensor_reduce(a_nmax[:, s, :], scA[:, s, :, 0:WIN + 1], AX.X, ALU.max, negate=True
                                      ).then_inc(max_ready, 1)
                else:
                    sc = pair(2 * s)
                    link(dve, dve.memset(sc[0:CHUNK, n * P + CHUNK:(n + 1) * P], -MASKED))
                    if k - 2 >= N_A:
                        dve.wait_ge(exp_done, k - 1)
                    dve.tensor_reduce(b_nmax[:, s:s + 1], sc[:, 0:(n + 1) * P], AX.X, ALU.max, negate=True
                                      ).then_inc(max_ready, 1)

            def pt_second(k):
                b, m, n = kind(k)
                s = k % 2
                ss = k % SUM_SLOTS
                dve.wait_ge(exp_done, k + 1)
                if b == "A":
                    link(dve, dve.reciprocal(a_rsum[:, ss, :], a_sum[:, ss, :]))
                else:
                    link(dve, dve.reciprocal(b_rsum[:, ss:ss + 1], b_sum[:, ss:ss + 1]))
                if not has_pt1(k):
                    return
                dve.wait_ge(pt1_done, pt1_count(k))
                if k >= 2:
                    dve.wait_ge(pv_done, k - 1)
                if b == "A":
                    dve.tensor_copy(ptA_half[s][0:CHUNK, :, :].rearrange("p g q -> p (g q)"), PS[0:CHUNK, 5, :]
                                    ).then_inc(pt1_ready, 1)
                else:
                    dve.tensor_copy(ptB[s][:, 4:n + 1, :].rearrange("p k q -> p (k q)"),
                                    PS[:, 5, 0:(n - 3) * P]).then_inc(pt1_ready, 1)

            def outputs(k):
                b, m, n = kind(k)
                ss = k % SUM_SLOTS
                dve.wait_ge(pv_done, k + 1)
                if b == "A":
                    o = yA[:, m, n * 256:(n + 1) * 256].rearrange("p (g c) -> p g c", c=A_DIM)
                    dve.tensor_tensor(o, PS[:, 6, 0:256].rearrange("p (g c) -> p g c", c=A_DIM),
                                      bcast(a_rsum[:, ss, :].rearrange("p (g o) -> p g o", o=1), [P, A_GROUP, A_DIM]),
                                      ALU.mult).then_inc(y_ready, 1)
                else:
                    dve.tensor_scalar(yB[:, n, m * V_DIM:(m + 1) * V_DIM], PS[:, 6, 0:V_DIM],
                                      b_rsum[:, ss:ss + 1], None, ALU.mult).then_inc(y_ready, 1)
            for k in range(N_UNITS + 2):
                if k == N_A:
                    maxima(k)
                    outputs(k - 2)
                    pt_second(k - 1)
                    outputs(k - 1)
                    group_vec(k)
                    continue
                if k < N_UNITS:
                    maxima(k)
                    group_vec(k)
                if k >= 2 and k != N_A + 1:
                    outputs(k - 2)
                if 1 <= k <= N_UNITS:
                    pt_second(k - 1)

            for n in range(16):
                j, h = n // 2, n % 2
                cols = slice(h * HALF, (h + 1) * HALF)
                dve.wait_ge(yT_hi_done, n + 1)
                dve.tensor_tensor(yT_lo[:, j, cols], PS[:, Y_BANKS[n % 8], :], yT_hi[:, j, cols], ALU.subtract
                                  ).then_inc(yT_ready, 1)

            def merge(i, first):
                for s in range(2):
                    d = 2 * i + s
                    dve.wait_ge(branch_done, 2 * d + 2)
                    dve.tensor_tensor(gated_a[:, :], pair(4 * s), gate[:, d, :], ALU.mult).then_inc(gated_step, 1)
                    dve.tensor_tensor(gated_b[:, :], pair(4 * s + 2), gate[:, d + KD, :], ALU.mult
                                      ).then_inc(gated_step, 1)
                    dve.wait_ge(gated_step, 2 * d + 2)
                    if not (first and s == 0):
                        dve.wait_ge(mT_hi_done, d)
                    dve.tensor_tensor(merged[:, :], gated_a[:, :], gated_b[:, :], ALU.add).then_inc(merged_ready, 1)
                    dve.wait_ge(mT_hi_done, d + 1)
                    dve.tensor_tensor(mT_lo[:, d, :], merged[:, :], mT_hi[:, d, :], ALU.subtract
                                      ).then_inc(mT_ready, 1)
            peeled(dve, KD // 2, merge)

            def x2_norm(t):
                if t % 4 == 0:
                    dve.wait_ge(x2_rstd_ready, t // 4 + 1)
                dve.tensor_scalar(x_norm[:, t, :], xr[:, t, :], x_rstd[:, t:t + 1], None, ALU.mult
                                  ).then_inc(x2_normed, 1)

            for n in range(2 * T):
                r, t = n // T, n % T
                dve.wait_ge(o_done, n + 1)
                if r == 0:
                    dve.wait_ge(xr_landed[t], 16)
                else:
                    dve.wait_ge(xr_added, T)
                dve.tensor_tensor(xr[:, t, :], pair(2 * (n % 4)), xr[:, t, :], ALU.add).then_inc(xr_added, 1)
                if r == 1 and t % 4 == 3:
                    h = t // 4
                    ts = slice(4 * h, 4 * h + 4)
                    dve.wait_ge(x2_squared, 4 * (h + 1))
                    dve.tensor_scalar(x_ms[:, ts], x_ss[:, ts], 1.0 / D, EPS, ALU.mult, ALU.add
                                      ).then_inc(x2_ms_ready, 1)
                if r == 1 and t in (5, 6):
                    x2_norm(2 * t - 10)
                    x2_norm(2 * t - 9)
            for t in range(4, T):
                x2_norm(t)
            for n in range(2 * KD):
                h, j = n // KD, n % KD
                cols = slice(h * HALF, (h + 1) * HALF)
                dve.wait_ge(h2T_hi_done, n + 1)
                dve.scalar_tensor_tensor(out=h2T_lo[:, j, cols], in0=PS[:, n % 8, :], scalar=g_mlp_c[:, j:j + 1],
                                         in1=h2T_hi[:, j, cols], op0=ALU.mult, op1=ALU.subtract
                                         ).then_inc(h2T_ready, 1)

            def ff_vec(g, first):
                for j in range(GROUP):
                    for h in range(2):
                        cols = slice(h * HALF, (h + 1) * HALF)
                        n = 8 * g + 2 * j + h
                        dve.wait_ge(relu_ready, n + 1)
                        if not (first and j == 0):
                            dve.wait_ge(uT_ready, n - 1)
                        dve.tensor_tensor(relu_sq[:, cols], relu_t[:, cols], relu_t[:, cols], ALU.mult
                                          ).then_inc(relu_sq_ready, 1)
                    for h in range(2):
                        cols = slice(h * HALF, (h + 1) * HALF)
                        n = 8 * g + 2 * j + h
                        dve.wait_ge(uT_hi_done, n + 1)
                        dve.tensor_tensor(uT_lo[:, j, cols], relu_sq[:, cols], uT_hi[:, j, cols], ALU.subtract
                                          ).then_inc(uT_ready, 1)
                for t in range(T):
                    dve.wait_ge(down_done, T * g + t + 1)
                    if t == 0 and not first:
                        dve.wait_ge(x3_added, T * g)
                    dve.tensor_tensor(xr[:, t, :], pair(4 + 2 * (t % 2)), xr[:, t, :], ALU.add
                                      ).then_inc(x3_added, 1)
            peeled(dve, FF_GROUPS, ff_vec)


_INS = ['x', 'positions', 'g_mix', 'w_in', 'b_gate', 'g_qa', 'g_ka', 'sinks_a', 'g_cq', 'g_ckv', 'w_uq', 'w_ukv',
        'g_qb', 'g_kb', 'w_branch_a', 'w_branch_b', 'w_out', 'g_mlp', 'w_ff1', 'w_ff2']


def kernel(**inputs):
    import concourse.bacc as bacc
    from concourse.bass_utils import run_bass_kernel_spmd

    nc = bacc.Bacc("TRN2", target_bir_lowering=False, num_devices=1)
    arrays, args = {}, []
    for name in _INS:
        a = np.ascontiguousarray(inputs[name])
        arrays["in_" + name] = a
        args.append(nc.dram_tensor("in_" + name, a.shape, mybir.dt.from_np(a.dtype), kind="ExternalInput").ap())
    args.append(nc.dram_tensor("out_0", (1, S, D), F32, kind="ExternalOutput").ap())
    build(nc, *args)
    r = run_bass_kernel_spmd(nc, [arrays], core_ids=[0])
    return r.results[0]["out_0"]
```
